# Optimizing a Trainium2 kernel written in Bass

```python
import math
import jax, jax.numpy as jnp
from jax import lax
import numpy as np

D_MODEL = 1024
BATCH = 1
SEQ = 256
DEPTH = 2

CHUNK = 64
Q_BLOCK = 128
HEAD_DIM = 64
N_HEADS_DIFF = 4
N_HEADS_SB = 4
N_HEADS_FOX = 4
DIFF_VDIM = 2 * HEAD_DIM
WIDTH_DIFF = N_HEADS_DIFF * DIFF_VDIM
WIDTH_SB = N_HEADS_SB * HEAD_DIM
WIDTH_FOX = N_HEADS_FOX * HEAD_DIM
N_BRANCH = 3
ROPE_THETA = 10000.0
N_EXPERTS = 8
TOP_K = 2
D_FF = 3584
ALPHA = (2 * DEPTH) ** 0.25
BETA = (8 * DEPTH) ** -0.25
N_DENSE = (DEPTH + 1) // 2
N_MOE = DEPTH // 2
SPLIT_SIZES = (
    N_HEADS_DIFF * 2 * HEAD_DIM,
    N_HEADS_DIFF * 2 * HEAD_DIM,
    WIDTH_DIFF,
    WIDTH_SB, WIDTH_SB, WIDTH_SB,
    WIDTH_FOX, WIDTH_FOX, WIDTH_FOX,
    N_HEADS_FOX,
    N_BRANCH * D_MODEL,
)
N_IN = sum(SPLIT_SIZES)

kernel_name = "hybrid_diff_stickbreak_fox_moe_deepnorm"

def layer_norm(x, g, b, eps=1e-5):
    xf = x.astype(jnp.float32)
    mu = jnp.mean(xf, axis=-1, keepdims=True)
    var = jnp.mean(jnp.square(xf - mu), axis=-1, keepdims=True)
    y = (xf - mu) * lax.rsqrt(var + eps) * g.astype(jnp.float32) + b.astype(jnp.float32)
    return y.astype(x.dtype)

def rms_norm(x, g, eps=1e-6):
    xf = x.astype(jnp.float32)
    y = xf * lax.rsqrt(jnp.mean(jnp.square(xf), axis=-1, keepdims=True) + eps) * g.astype(jnp.float32)
    return y.astype(x.dtype)

def rope(x, pos):
    half = x.shape[-1] // 2
    inv = ROPE_THETA ** (-jnp.arange(half, dtype=jnp.float32) / half)
    ang = pos[:, None] * inv[None, :]
    cos, sin = jnp.cos(ang), jnp.sin(ang)
    xf = x.astype(jnp.float32)
    x1, x2 = xf[..., :half], xf[..., half:]
    return jnp.concatenate([x1 * cos - x2 * sin, x2 * cos + x1 * sin], axis=-1).astype(x.dtype)

def _heads(t, n_heads, d):
    B, S, _ = t.shape
    return t.reshape(B, S, n_heads, d).transpose(0, 2, 1, 3)

def _merge_heads(o):
    B, H, S, d = o.shape
    return o.transpose(0, 2, 1, 3).reshape(B, S, H * d)

def _q_blocks(q):
    B, H, S, d = q.shape
    return q.reshape(B, H, S // Q_BLOCK, Q_BLOCK, d).transpose(2, 0, 1, 3, 4)

def _from_blocks(o):
    n, B, H, QB, d = o.shape
    return o.transpose(1, 2, 0, 3, 4).reshape(B, H, n * QB, d)

def diff_attention(q, k, v, lam):
    B, H, _, S, d = q.shape
    n_blk = S // Q_BLOCK
    k_chunk = jnp.arange(S) // CHUNK
    q_blk = q.reshape(B, H, 2, n_blk, Q_BLOCK, d).transpose(3, 0, 1, 2, 4, 5)
    scale = d ** -0.5

    def body(args):
        qb, i = args
        q_chunk = (i * Q_BLOCK + jnp.arange(Q_BLOCK)) // CHUNK
        mask = k_chunk[None, :] <= q_chunk[:, None]
        s = jnp.einsum('bhmqd,bhmkd->bhmqk', qb, k).astype(jnp.float32) * scale
        p = jax.nn.softmax(jnp.where(mask, s, -jnp.inf), axis=-1)
        w = p[:, :, 0] - lam * p[:, :, 1]
        return jnp.einsum('bhqk,bhkv->bhqv', w.astype(v.dtype), v)

    o = lax.map(body, (q_blk, jnp.arange(n_blk)))
    return o.transpose(1, 2, 0, 3, 4).reshape(B, H, S, v.shape[-1])

def stick_breaking_attention(q, k, v):
    B, H, S, d = q.shape
    n_blk = S // Q_BLOCK
    k_pos = jnp.arange(S)
    scale = d ** -0.5

    def body(args):
        qb, i = args
        q_pos = i * Q_BLOCK + jnp.arange(Q_BLOCK)
        mask = k_pos[None, :] < q_pos[:, None]
        z = jnp.einsum('bhqd,bhkd->bhqk', qb, k).astype(jnp.float32) * scale
        u = jnp.where(mask, jax.nn.softplus(z), 0.0)
        suffix = lax.cumsum(u, axis=u.ndim - 1, reverse=True) - u
        log_a = -jax.nn.softplus(-z) - suffix
        a = jnp.where(mask, jnp.exp(jnp.where(mask, log_a, -jnp.inf)), 0.0)
        return jnp.einsum('bhqk,bhkd->bhqd', a.astype(v.dtype), v)

    return _from_blocks(lax.map(body, (_q_blocks(q), jnp.arange(n_blk))))

def forgetting_attention(q, k, v, log_f):
    B, H, S, d = q.shape
    n_blk = S // Q_BLOCK
    k_pos = jnp.arange(S)
    scale = d ** -0.5
    F = jnp.cumsum(log_f, axis=-1)
    F_blk = F.reshape(B, H, n_blk, Q_BLOCK).transpose(2, 0, 1, 3)

    def body(args):
        qb, fq, i = args
        q_pos = i * Q_BLOCK + jnp.arange(Q_BLOCK)
        mask = k_pos[None, :] <= q_pos[:, None]
        s = jnp.einsum('bhqd,bhkd->bhqk', qb, k).astype(jnp.float32) * scale
        s = s + fq[..., :, None] - F[:, :, None, :]
        p = jax.nn.softmax(jnp.where(mask, s, -jnp.inf), axis=-1)
        return jnp.einsum('bhqk,bhkd->bhqd', p.astype(v.dtype), v)

    return _from_blocks(lax.map(body, (_q_blocks(q), F_blk, jnp.arange(n_blk))))

def token_mixers(h, layer, w_in, b_forget, lam_q1, lam_k1, lam_q2, lam_k2, diff_norm_g,
                 w_up_diff, w_up_sb, w_up_fox, w_out):
    B, S, D = h.shape
    pos = jnp.arange(S, dtype=jnp.float32)
    proj = h @ w_in
    offsets = [int(c) for c in np.cumsum(SPLIT_SIZES)[:-1]]
    (dq, dk, dv, sq, sk, sv, fq, fk, fv, f_logit, g_logit) = jnp.split(proj, offsets, axis=-1)

    dq = rope(dq.reshape(B, S, N_HEADS_DIFF, 2, HEAD_DIM).transpose(0, 2, 3, 1, 4), pos)
    dk = rope(dk.reshape(B, S, N_HEADS_DIFF, 2, HEAD_DIM).transpose(0, 2, 3, 1, 4), pos)
    lam_init = 0.8 - 0.6 * math.exp(-0.3 * layer)
    f32 = jnp.float32
    lam = (jnp.exp(jnp.sum(lam_q1.astype(f32) * lam_k1.astype(f32)))
           - jnp.exp(jnp.sum(lam_q2.astype(f32) * lam_k2.astype(f32))) + lam_init)
    o_diff = diff_attention(dq, dk, _heads(dv, N_HEADS_DIFF, DIFF_VDIM), lam)
    o_diff = _merge_heads(rms_norm(o_diff, diff_norm_g) * (1.0 - lam_init))

    o_sb = _merge_heads(stick_breaking_attention(
        _heads(sq, N_HEADS_SB, HEAD_DIM), _heads(sk, N_HEADS_SB, HEAD_DIM),
        _heads(sv, N_HEADS_SB, HEAD_DIM)))

    log_f = jax.nn.log_sigmoid(f_logit.astype(f32) + b_forget.astype(f32)).transpose(0, 2, 1)
    o_fox = _merge_heads(forgetting_attention(
        _heads(fq, N_HEADS_FOX, HEAD_DIM), _heads(fk, N_HEADS_FOX, HEAD_DIM),
        _heads(fv, N_HEADS_FOX, HEAD_DIM), log_f))

    gates = jax.nn.sigmoid(g_logit.reshape(B, S, N_BRANCH, D))
    merged = (gates[:, :, 0] * (o_diff @ w_up_diff)
              + gates[:, :, 1] * (o_sb @ w_up_sb)
              + gates[:, :, 2] * (o_fox @ w_up_fox))
    return merged @ w_out

def swiglu(h, w_gate, w_up, w_down):
    return (jax.nn.silu(h @ w_gate) * (h @ w_up)) @ w_down

def moe_ffn(h, w_router, b_router, w_gate, w_up, w_down):
    B, S, D = h.shape
    hf = h.reshape(B * S, D)
    logits = (hf @ w_router).astype(jnp.float32) + b_router.astype(jnp.float32)
    top_v, top_i = lax.top_k(logits, TOP_K)
    top_w = jax.nn.softmax(top_v, axis=-1)
    combine = jnp.sum(jax.nn.one_hot(top_i, N_EXPERTS, dtype=jnp.float32) * top_w[..., None], axis=1)
    combine = combine.astype(h.dtype)
    out = jnp.zeros_like(hf)
    for e in range(N_EXPERTS):
        out = out + combine[:, e:e + 1] * swiglu(hf, w_gate[e], w_up[e], w_down[e])
    return out.reshape(B, S, D)

def setup_inputs(seed: int = 0) -> dict:
    key = jax.random.key(seed)
    ks = jax.random.split(key, 32)
    f32 = jnp.float32
    n = lambda k, shape: jax.random.normal(k, shape, dtype=f32)
    D = D_MODEL
    col_scale = np.concatenate([
        np.full(SPLIT_SIZES[0] + SPLIT_SIZES[1], 1.0, np.float32),
        np.full(SPLIT_SIZES[2], BETA, np.float32),
        np.full(2 * WIDTH_SB, 1.0, np.float32), np.full(WIDTH_SB, BETA, np.float32),
        np.full(2 * WIDTH_FOX, 1.0, np.float32), np.full(WIDTH_FOX, BETA, np.float32),
        np.full(N_HEADS_FOX + N_BRANCH * D, 1.0, np.float32)])
    return {
        "x": n(ks[0], (BATCH, SEQ, D)),
        "ln_in_g": 1.0 + 0.05 * n(ks[1], (D,)),
        "ln_in_b": 0.02 * n(ks[2], (D,)),
        "w_in": n(ks[3], (DEPTH, D, N_IN)) * (D ** -0.5) * jnp.asarray(col_scale),
        "b_forget": 3.0 + 0.5 * n(ks[4], (DEPTH, N_HEADS_FOX)),
        "lam_q1": 0.1 * n(ks[5], (DEPTH, HEAD_DIM)),
        "lam_k1": 0.1 * n(ks[6], (DEPTH, HEAD_DIM)),
        "lam_q2": 0.1 * n(ks[7], (DEPTH, HEAD_DIM)),
        "lam_k2": 0.1 * n(ks[8], (DEPTH, HEAD_DIM)),
        "diff_norm_g": 1.0 + 0.05 * n(ks[9], (DEPTH, DIFF_VDIM)),
        "w_up_diff": n(ks[10], (DEPTH, WIDTH_DIFF, D)) * (WIDTH_DIFF ** -0.5) * BETA,
        "w_up_sb": n(ks[11], (DEPTH, WIDTH_SB, D)) * (WIDTH_SB ** -0.5) * BETA,
        "w_up_fox": n(ks[12], (DEPTH, WIDTH_FOX, D)) * (WIDTH_FOX ** -0.5) * BETA,
        "w_out": n(ks[13], (DEPTH, D, D)) * (D ** -0.5) * BETA,
        "ln_mix_g": 1.0 + 0.05 * n(ks[14], (DEPTH, D)),
        "ln_mix_b": 0.02 * n(ks[15], (DEPTH, D)),
        "ln_ffn_g": 1.0 + 0.05 * n(ks[16], (DEPTH, D)),
        "ln_ffn_b": 0.02 * n(ks[17], (DEPTH, D)),
        "w_gate_dense": n(ks[18], (N_DENSE, D, D_FF)) * (D ** -0.5),
        "w_up_dense": n(ks[19], (N_DENSE, D, D_FF)) * (D ** -0.5) * BETA,
        "w_down_dense": n(ks[20], (N_DENSE, D_FF, D)) * (D_FF ** -0.5) * BETA,
        "w_router": n(ks[21], (N_MOE, D, N_EXPERTS)) * (D ** -0.5),
        "b_router": 0.01 * n(ks[22], (N_MOE, N_EXPERTS)),
        "w_gate_moe": n(ks[23], (N_MOE, N_EXPERTS, D, D_FF)) * (D ** -0.5),
        "w_up_moe": n(ks[24], (N_MOE, N_EXPERTS, D, D_FF)) * (D ** -0.5) * BETA,
        "w_down_moe": n(ks[25], (N_MOE, N_EXPERTS, D_FF, D)) * (D_FF ** -0.5) * BETA,
    }

def reference(x, ln_in_g, ln_in_b, w_in, b_forget, lam_q1, lam_k1, lam_q2, lam_k2,
              diff_norm_g, w_up_diff, w_up_sb, w_up_fox, w_out, ln_mix_g, ln_mix_b,
              ln_ffn_g, ln_ffn_b, w_gate_dense, w_up_dense, w_down_dense, w_router,
              b_router, w_gate_moe, w_up_moe, w_down_moe):
    h = layer_norm(x, ln_in_g, ln_in_b)
    for l in range(DEPTH):
        y = token_mixers(h, l, w_in[l], b_forget[l], lam_q1[l], lam_k1[l], lam_q2[l],
                         lam_k2[l], diff_norm_g[l], w_up_diff[l], w_up_sb[l], w_up_fox[l],
                         w_out[l])
        h = layer_norm(ALPHA * h + y, ln_mix_g[l], ln_mix_b[l])
        if l % 2 == 0:
            j = l // 2
            y = swiglu(h, w_gate_dense[j], w_up_dense[j], w_down_dense[j])
        else:
            j = l // 2
            y = moe_ffn(h, w_router[j], b_router[j], w_gate_moe[j], w_up_moe[j], w_down_moe[j])
        h = layer_norm(ALPHA * h + y, ln_ffn_g[l], ln_ffn_b[l])
    return h


_drawn_inputs = setup_inputs


def setup_inputs(seed=0):
    import zlib

    import numpy as np

    out = dict(_drawn_inputs(seed))
    spreads = {}
    factors = {'b_forget': 63.664,
     'lam_q1': 7.364,
     'lam_k1': 2.983,
     'lam_q2': 5.02,
     'lam_k2': 6.701,
     'diff_norm_g': 8.0,
     'b_router': 23.538,
     'w_up_fox': 2.863}
    for name, (base, spread) in spreads.items():
        noise = np.random.default_rng([zlib.crc32(name.encode()), seed]).standard_normal(out[name].shape)
        drawn = base * np.exp(spread * noise) if base else spread * noise
        out[name] = __import__('jax').numpy.asarray(drawn.astype(out[name].dtype))
    for name, factor in factors.items():
        out[name] = (out[name] * factor).astype(out[name].dtype)
    return out
```

```python
import math
from contextlib import ExitStack

import numpy as np

import concourse.bass as bass
from concourse import mybir

F32 = mybir.dt.float32
F32R = mybir.dt.float32r
I32 = mybir.dt.int32
ALU = mybir.AluOpType
ACT = mybir.ActivationFunctionType
AX = mybir.AxisListType.X

P = 128
D = 1024
SEQ = 256
DEPTH = 2
TILES = SEQ // P
KT = D // P
CHUNK = 64
HD = 64
N_EXP = 8
D_FF = 3584
FC = D_FF // 512
ALPHA = (2 * DEPTH) ** 0.25
QKV = 3072
NF = 4
NEG = -1e30
ITEMS = N_EXP + SEQ * 2 // (P + 1)
ITEM_COLS = ITEMS + 1

RING, HRING = 6, 3
MIX_UNITS, ITEM_UNITS = 36, 6 * FC
DENSE_ITEMS = TILES
LAYER_UNITS = MIX_UNITS + DENSE_ITEMS * ITEM_UNITS
U_F, U_GATE, U_UP, U_OUT = 12, 14, 26, 32

GROUPS = [("diff", 1), ("sb", 1), ("fox", 1), ("diff", 0), ("sb", 0), ("fox", 0)]
BANK = [2, 2, 4, 2, 4, 2]
Q_BLK = {"diff": 0, "sb": 8, "fox": 12}
K_BLK = {"diff": 4, "sb": 10, "fox": 14}
CAT_OFF = {"diff": 0, "sb": 512, "fox": 768}
FREED_BY = [0, 1, 1, 2, 3, 4]
ROUNDS_BEFORE = [0, 2, 4, 6, 7, 8]
ROUNDS = 9

_c = {}
_at = 0
for _name, _n in (("ident", P), ("tri", TILES * SEQ), ("iota", P), ("mfox1", 256), ("mfox0", 128),
                  ("mdiff1", 256), ("mdiff0", 128), ("msb1", 256), ("msb0", 128),
                  ("cos", TILES * HD), ("sin", TILES * HD), ("negsel", NF * P),
                  ("drk", TILES * ITEM_COLS), ("layer", DEPTH * 4), ("iota8", N_EXP),
                  ("first", N_EXP), ("expert", ITEM_COLS)):
    _c[_name] = (_at, _at + _n)
    _at += _n
N_CONST = _at
PARAM_LOADS = 5
COLS = dict(_c)


def mix_words(k):
    if U_F <= k < U_GATE:
        return 4 * NF
    return 1024 if U_UP <= k < U_OUT and (k - U_UP) % 3 else 2048


def constants():
    c = np.zeros((P, N_CONST), np.float32)

    def put(name, value):
        a, b = COLS[name]
        c[:, a:b] = np.broadcast_to(value, (P, b - a))

    p = np.arange(P)
    s = np.arange(SEQ)
    put("ident", np.eye(P))
    put("tri", np.concatenate([(p[:, None] + P * k <= s[None, :]) for k in range(TILES)], 1))
    put("iota", p[None, :])
    for t, n in ((1, 256), (0, 128)):
        q = p[:, None] + P * t
        k = np.arange(n)[None, :]
        put(f"mfox{t}", np.where(k <= q, 0.0, NEG))
        put(f"mdiff{t}", np.where(k // CHUNK <= q // CHUNK, 0.0, NEG))
        put(f"msb{t}", np.where(k < q, 0.0, NEG))
    half = HD // 2
    inv = (np.float32(10000.0) ** (-np.arange(half, dtype=np.float32) / np.float32(half))).astype(np.float32)
    ang = (s.astype(np.float32)[:, None] * inv[None, :]).astype(np.float32)
    cos, sin = np.cos(ang), np.sin(ang)
    put("cos", np.concatenate([np.tile(cos[P * t:P * t + P], (1, 2)) for t in range(TILES)], 1))
    put("sin", np.concatenate([np.concatenate([-sin[P * t:P * t + P], sin[P * t:P * t + P]], 1) for t in range(TILES)], 1))
    put("negsel", np.repeat(-np.eye(P, NF), P, axis=1))
    drk = np.full((P, TILES, ITEM_COLS), -1.0)
    for t in range(TILES):
        drk[:, t, t] = p
    put("drk", drk.reshape(P, -1))
    lam = [0.8 - 0.6 * math.exp(-0.3 * l) for l in range(DEPTH)]
    put("layer", np.array([[lam[l], 1.0 - lam[l], l % 2, 1 - l % 2] for l in range(DEPTH)]).reshape(1, -1))
    put("iota8", np.arange(N_EXP)[None, :])
    put("first", np.arange(N_EXP)[None, :] - 99.0)
    put("expert", np.array([1.0 + i if i < N_EXP else 0.0 for i in range(ITEM_COLS)])[None, :])
    return c


def build(nc, x, consts, ln_in, w_in, b_forget, lam_qk, diff_g, w_up_diff, w_up_sb, w_up_fox, w_out,
          ln_mix, ln_ffn, w_router, b_router, w_gate, w_up, w_down, out):
    with ExitStack() as ctx:
        cursor = [17 * 1024]

        def at(name, shape, dt, offset):
            return nc.alloc_sbuf_tensor_at(name, shape, dt, offset=offset)

        def place(name, shape, dt=F32):
            offset = cursor[0]
            cursor[0] += (int(np.prod(shape[1:])) * 4 + 31) // 32 * 32
            return at(name, shape, dt, offset)

        raw_at = cursor[0]
        raw = place("raw", [P, RING, 2048])
        w_lo = at("w_lo", [P, RING, 2048], F32R, raw_at)
        w_hi = place("w_hi", [P, HRING, 2048], F32R)
        h = place("h", [P, TILES, D])
        act_hi = place("act_hi", [P, KT, SEQ], F32R)
        act_lo = place("act_lo", [P, KT, SEQ], F32R)
        cst = place("cst", [P, N_CONST])
        cat = place("cat", [P, TILES, D])
        small = place("small", [P, 1300])
        shared_at = cursor[0]
        gates = place("gates", [P, TILES, 3, D])
        v_sb = place("v_sb", [P, TILES, D])
        qkT_at = cursor[0]
        qkT = place("qkT", [P, 16, SEQ])
        p_at = cursor[0]
        prob_even = place("prob_even", [P, 2048])
        prob_odd = place("prob_odd", [P, 1024])
        sb_tmp = place("sb_tmp", [P, 1024])
        wT = place("wT", [P, 2, 4, P])
        sq = place("sq", [P, 512])
        q_stage = at("q_stage", [P, 2, TILES, 512], F32, p_at)
        end_mixer = cursor[0]
        mrg_hi = at("mrg_hi", [P, KT, SEQ], F32R, qkT_at)
        mrg_lo = at("mrg_lo", [P, KT, SEQ], F32R, qkT_at + KT * SEQ * 4)
        ln_gb = at("ln_gb", [P, 2, D], F32, p_at)
        cursor[0] = shared_at
        x_hi = place("x_hi", [P, KT, P], F32R)
        x_lo = place("x_lo", [P, KT, P], F32R)
        sig = place("sig", [P, 512])
        gsig = place("gsig", [P, 512])
        hid = place("hid", [P, 512])
        hid_hi = place("hid_hi", [P, 4, P], F32R)
        hid_lo = place("hid_lo", [P, 4, P], F32R)
        d_sb = place("d_sb", [P, D])
        scat = place("scat", [P, TILES, P])
        gath = place("gath", [P, TILES, P])
        rt = place("rt", [P, 512])
        assert cursor[0] <= qkT_at and end_mixer <= 229344

        zero_w = ctx.enter_context(nc.sbuf_tensor("zero_w", [P, P], F32R))

        def c(name, n=None, **dims):
            a, b = COLS[name]
            return cst[:, a:b]

        ident = c("ident")
        iota = c("iota")
        tri = c("tri").rearrange("p (k s) -> p k s", k=TILES)

        used = [0]

        def scratch(n, *dims):
            a = used[0]
            used[0] += n
            return small[:, a:a + n]

        lamq = scratch(DEPTH * 4 * HD).rearrange("p (l m d) -> p l m d", l=DEPTH, m=4)
        diffg = scratch(P)
        bf2 = scratch(DEPTH * NF).rearrange("p (l f) -> p l f", l=DEPTH)
        diffg2 = scratch(DEPTH * P).rearrange("p (l f) -> p l f", l=DEPTH)
        b_rt = scratch(N_EXP)
        bf = scratch(NF)
        lam_s = scratch(4)
        lam_e = scratch(4)
        lam = scratch(DEPTH)
        neg_lam = scratch(1)
        lay = scratch(4)
        mv = scratch(TILES * 2).rearrange("p (t m) -> p t m", t=TILES)
        bst = scratch(12).rearrange("p (c m) -> p c m", c=2)
        rv = scratch(4)
        rr = scratch(4)
        rn = scratch(4)
        f_x = scratch(8)
        f_l = scratch(8)
        lf = scratch(8).rearrange("p (t m) -> p t m", t=TILES)
        f_col = scratch(8).rearrange("p (t m) -> p t m", t=TILES)
        negmax = scratch(8)
        psum_s = scratch(8)
        rsum = scratch(8)
        f_row = scratch(SEQ)
        assert used[0] <= 1300

        rused = [0]

        def route(n):
            a = rused[0]
            rused[0] += n
            return rt[:, a:a + n]

        lg = route(16).rearrange("p (t e) -> p t e", t=TILES)
        lg2 = route(16).rearrange("p (t e) -> p t e", t=TILES)
        eq = route(16).rearrange("p (t e) -> p t e", t=TILES)
        oh1 = route(16).rearrange("p (t e) -> p t e", t=TILES)
        oh2 = route(16).rearrange("p (t e) -> p t e", t=TILES)
        sel = route(16).rearrange("p (t e) -> p t e", t=TILES)
        cwe = route(16).rearrange("p (t e) -> p t e", t=TILES)
        rkm = route(16).rearrange("p (t e) -> p t e", t=TILES)
        m1 = route(2).rearrange("p (t e) -> p t e", t=TILES)
        m2 = route(2).rearrange("p (t e) -> p t e", t=TILES)
        fi = route(2).rearrange("p (t e) -> p t e", t=TILES)
        dd = route(2).rearrange("p (t e) -> p t e", t=TILES)
        ee = route(2).rearrange("p (t e) -> p t e", t=TILES)
        w1 = route(2).rearrange("p (t e) -> p t e", t=TILES)
        w2 = route(2).rearrange("p (t e) -> p t e", t=TILES)
        ov = route(N_EXP)
        inc = route(N_EXP)
        exc = route(N_EXP)
        osel = route(N_EXP)
        prod = route(16).rearrange("p (t e) -> p t e", t=TILES)
        tab_rk = route(TILES * ITEM_COLS).rearrange("p (t i) -> p t i", t=TILES)
        tab_cw = route(TILES * ITEM_COLS).rearrange("p (t i) -> p t i", t=TILES)
        item_rk = route(TILES * ITEM_COLS).rearrange("p (t i) -> p t i", t=TILES)
        item_cw = route(TILES * (ITEM_COLS + 1)).rearrange("p (t i) -> p t i", t=TILES)
        ftab = route(ITEM_COLS + 1)
        wrb = route(N_EXP)
        assert rused[0] <= 512
        itab = ctx.enter_context(nc.sbuf_tensor("itab", [P, 16], I32))
        w_rt = ctx.enter_context(nc.sbuf_tensor("w_rt", [P, KT, N_EXP], F32))

        ps = ctx.enter_context(nc.psum_tensor("ps", [P, 8, 512], F32))

        def sem(name):
            return ctx.enter_context(nc.semaphore(name))

        s_raw = [sem(f"raw_loaded_{s}") for s in range(RING)]
        s_hi = sem("hi_split")
        s_lo = sem("lo_split")
        s_used = sem("unit_used")
        s_cst = sem("const_loaded")
        s_par = sem("params_loaded")
        s_x = sem("x_loaded")
        s_gb = sem("ln_params_loaded")
        s_lnd = sem("ln_params_used")
        s_h = sem("h_ready")
        s_tp = sem("transposed")
        s_tph = sem("transposed_hi")
        s_tpl = sem("transposed_lo")
        s_rv = sem("variance_ready")
        s_rr = sem("rsqrt_seeded")
        s_lam = sem("lambda_sums")
        s_lame = sem("lambda_exps")
        s_rope = sem("rope_done")
        s_qev = sem("qkv_copied")
        s_qt = sem("qk_transposed")
        s_qte = sem("qk_copied")
        s_fx = sem("forget_logit")
        s_fln = sem("forget_softplus")
        s_lf = sem("log_forget")
        s_F = sem("forget_sums")
        s_Fr = sem("forget_row_copied")
        s_Fc = sem("forget_col_copied")
        s_sc = sem("scores_done")
        s_scr = sem("scores_read")
        s_sbl = sem("sb_log_done")
        s_ei = sem("exp_input")
        s_ex = sem("exp_done")
        s_w = sem("weights_ready")
        s_wt = sem("weights_transposed")
        s_wte = sem("weights_copied")
        s_pv = sem("pv_done")
        s_pve = sem("pv_copied")
        s_rms = sem("rms_done")
        s_gl = sem("gate_logits_copied")
        s_sg = sem("gates_done")
        s_gm = sem("branches_gated")
        s_mrg = sem("merged")
        s_lg = sem("router_logits")
        s_rd = sem("router_gap")
        s_re = sem("router_exp")
        s_sel = sem("experts_selected")
        s_rk = sem("ranks_summed")
        s_tab = sem("items_listed")
        s_S = sem("gather_matrix")
        s_ga = sem("tokens_gathered")
        s_xh = sem("gathered_hi")
        s_xl = sem("gathered_lo")
        s_sig = sem("sigmoid_done")
        s_gs = sem("gate_silu")
        s_hd = sem("hidden_ready")
        s_tr = sem("hidden_transposed")
        s_th = sem("hidden_hi")
        s_tl = sem("hidden_lo")
        s_dA = sem("down_copied_left")
        s_dV = sem("down_copied_right")
        s_sT = sem("scatter_transposed")
        s_sTe = sem("scatter_copied")
        s_cb = sem("item_scattered")
        s_ac = sem("item_added")
        s_dch = sem("vector_chain")
        s_ach = sem("scalar_chain")
        s_zero = sem("zeros_ready")
        s_passed = sem("waits_passed")
        s_out = sem("output_stored")

        DVE_LAYER = 138
        ACT_LAYER = 10

        def hold(eng, semaphore, value):
            eng.wait_ge(semaphore, value)
            eng.sem_inc(s_passed, 1)

        def groups_of(kind, t):
            return (8 if kind == "diff" else 4), P * (t + 1)

        def place_of(g, j):
            return j % 2 * (groups_of(*GROUPS[g])[0] // 2) + j // 2

        def scores_of(g):
            m, keys = groups_of(*GROUPS[g])
            half = m * keys // 2
            if half >= 512:
                return ps[:, BANK[g]:BANK[g] + half // 256, :].rearrange("p (a b) n -> p a (b n)", a=2)
            return ps[:, BANK[g]:BANK[g] + 2, 0:half]

        def prob(g):
            return (prob_odd if g % 2 else prob_even)

        block = ctx.enter_context(nc.Block())

        @block.sync
        def _(sp):
            sp.dma_start(cst[:], consts[:, :]).then_inc(s_cst, 16)
            sp.dma_start(h[:], x[0].rearrange("(t p) d -> p t d", p=P)).then_inc(s_x, 16)

            def load(base, k, src, n):
                hold(sp, s_used, base + (k + 1))
                a = src.shape[1]
                dst = raw[:, k % RING, 0:n].rearrange("p (a n) -> p a n", a=a)
                sp.dma_start(dst, src).then_inc(s_raw[k % RING], 16)

            def rows(w, l, r0, r1, c0, c1):
                return w[bass.ds(l, 1), r0:r1, c0:c1].rearrange("a (k p) n -> p (a k) n", p=P)

            def item_units(base, e, ks):
                for k in ks:
                    kk, f = (k, 0) if k < 4 else ((k - 4) % 6, 1 + (k - 4) // 6)
                    if f == FC:
                        kk += 4
                    if kk < 4:
                        w = w_gate if kk < 2 else w_up
                        r = 512 * (kk % 2)
                        load(base, k, rows(w, e, r, r + 512, 512 * f, 512 * f + 512), 2048)
                    else:
                        r = 512 * (f - 1) + 256 * (kk - 4)
                        load(base, k, rows(w_down, e, r, r + 256, 0, D), 2048)

            with sp.Fori(0, DEPTH) as l:
                base = l * LAYER_UNITS
                for cc in range(6):
                    for hk in range(2):
                        load(base, 2 * cc + hk, rows(w_in, l, 512 * hk, 512 * hk + 512, 512 * cc, 512 * cc + 512), 2048)
                for hk in range(2):
                    load(base, U_F + hk, rows(w_in, l, 512 * hk, 512 * hk + 512, QKV, QKV + NF), 4 * NF)
                for cc in range(6):
                    c0 = QKV + NF + 512 * cc
                    for hk in range(2):
                        load(base, U_GATE + 2 * cc + hk, rows(w_in, l, 512 * hk, 512 * hk + 512, c0, c0 + 512), 2048)
                for cc in range(2):
                    for b, (w, r) in enumerate(((w_up_diff, 512), (w_up_sb, 256), (w_up_fox, 256))):
                        load(base, U_UP + 3 * cc + b, rows(w, l, 0, r, 512 * cc, 512 * cc + 512), 4 * r)
                for cc in range(2):
                    for hk in range(2):
                        load(base, U_OUT + 2 * cc + hk, rows(w_out, l, 512 * hk, 512 * hk + 512, 512 * cc, 512 * cc + 512), 2048)
                first = base + MIX_UNITS
                item_units(first, l, range(6))
                hold(sp, s_tab, l + 1)
                n = sp.value_load(itab[0:1, 0:1], min_val=2, max_val=ITEMS)
                with sp.Fori(0, n - 1) as i:
                    ib = l * LAYER_UNITS + i * ITEM_UNITS + MIX_UNITS
                    e = sp.value_load(itab[0:1, bass.ds(i + 1, 1)], min_val=0, max_val=N_EXP)
                    item_units(ib, e, range(6, ITEM_UNITS))
                    e2 = sp.value_load(itab[0:1, bass.ds(i + 2, 1)], min_val=0, max_val=N_EXP)
                    item_units(ib + ITEM_UNITS, e2, range(6))
                e = sp.value_load(itab[0:1, bass.ds(n, 1)], min_val=0, max_val=N_EXP)
                item_units(l * LAYER_UNITS + (n - 1) * ITEM_UNITS + MIX_UNITS, e, range(6, ITEM_UNITS))
            n = sp.value_load(itab[0:1, 0:1], min_val=2, max_val=ITEMS)
            for k in range(HRING):
                load(LAYER_UNITS + MIX_UNITS + n * ITEM_UNITS, k, rows(w_in, 0, 0, 512, 0, 512), 2048)
            sp.wait_ge(s_h, TILES * (1 + 2 * DEPTH))
            sp.dma_start(out[0].rearrange("(t p) d -> p t d", p=P), h[:]).then_inc(s_out, 16)
            sp.wait_ge(s_out, 16)

        @block.gpsimd
        def _(pool):
            nc.gpsimd.memset(zero_w[:].bitcast(F32), 0.0).then_inc(s_zero, 1)
            pool.dma_start(lamq, lam_qk.rearrange("(o l) m d -> o l m d", o=1).to_broadcast([P, DEPTH, 4, HD])).then_inc(s_par, 16)
            pool.dma_start(bf2, b_forget.rearrange("(o l) f -> o l f", o=1).to_broadcast([P, DEPTH, NF])).then_inc(s_par, 16)
            pool.dma_start(diffg2, diff_g.rearrange("(o l) f -> o l f", o=1).to_broadcast([P, DEPTH, P])).then_inc(s_par, 16)
            pool.dma_start(b_rt, b_router.to_broadcast([P, N_EXP])).then_inc(s_par, 16)
            pool.dma_start(w_rt[:], w_router[0].rearrange("(k p) e -> p k e", p=P)).then_inc(s_par, 16)
            pool.dma_start(ln_gb[:], ln_in.rearrange("(o m) d -> o m d", o=1).to_broadcast([P, 2, D])).then_inc(s_gb, 16)
            with pool.Fori(0, DEPTH) as l:
                hold(pool, s_tpl, l * 16 + 8)
                pool.dma_start(ln_gb[:], ln_mix[bass.ds(l, 1)].to_broadcast([P, 2, D])).then_inc(s_gb, 16)
                hold(pool, s_lnd, l * 2 + 2)
                pool.dma_start(ln_gb[:], ln_ffn[bass.ds(l, 1)].to_broadcast([P, 2, D])).then_inc(s_gb, 16)

        @block.scalar
        def _(act):
            link_count = [0, 0]

            def link(ins):
                link_count[1] += 1
                ins.then_inc(s_ach, 1)
                act.wait_ge(s_ach, link_count[0] + link_count[1])

            def split(nb, qb, k, n=2048):
                act.wait_ge(s_raw[k % RING], (qb + (k // RING + 1)) * 16)
                act.wait_ge(s_used, nb + (k + RING - HRING + 1))
                nc.scalar.activation(w_hi[:, k % HRING, 0:n], raw[:, k % RING, 0:n], ACT.Copy).then_inc(s_hi, 1)

            def rsqrt_seed(index, n):
                act.wait_ge(s_rv, index + 1)
                link(nc.scalar.activation(rr[:, 0:n], rv[:, 0:n], ACT.Ln))
                nc.scalar.activation(rr[:, 0:n], rr[:, 0:n], ACT.Exp, scale=-0.5).then_inc(s_rr, 1)

            def transposed_hi(job, hi):
                for step in range(4):
                    t, half = step // 2, step % 2
                    act.wait_ge(s_tp, job * 4 + (step + 1))
                    nc.scalar.activation(hi[:, 4 * half:4 * half + 4, t * P:t * P + P],
                                         ps[:, 2 + step, :].rearrange("p (k n) -> p k n", k=4),
                                         ACT.Copy).then_inc(s_tph, 1)

            nc.scalar.sem_inc(s_dA, 1)
            nc.scalar.sem_inc(s_sTe, 1)
            for k in range(HRING):
                split(0, 0, k)
            act.wait_ge(s_lam, 1)
            nc.scalar.activation(lam_e, lam_s, ACT.Exp).then_inc(s_lame, 1)
            rsqrt_seed(0, TILES)
            transposed_hi(0, act_hi)

            with act.Fori(0, DEPTH) as l:
                nb, qb = l * LAYER_UNITS, l * (LAYER_UNITS // RING)
                link_count[0], link_count[1] = l * ACT_LAYER + 1, 0

                def qk_copy(j):
                    act.wait_ge(s_qt, l * 5 + (j + 1))
                    parts = {0: [(0, 4, 0.125)], 1: [(4, 4, 1.0)], 2: [(8, 2, 0.125), (10, 2, 1.0)],
                             3: [(12, 2, 0.125)], 4: [(14, 2, 1.0)]}[j]
                    for t in range(TILES):
                        for b0, nblk, scale in parts:
                            o = (b0 - parts[0][0]) * P
                            ins = nc.scalar.activation(
                                qkT[:, b0:b0 + nblk, t * P:t * P + P],
                                ps[:, 4 + t, o:o + nblk * P].rearrange("p (b n) -> p b n", b=nblk),
                                ACT.Copy, scale=scale)
                    ins.then_inc(s_qte, 1)

                for cc in range(6):
                    split(nb, qb, 2 * cc + 3, mix_words(2 * cc + 3))
                    split(nb, qb, 2 * cc + 4, mix_words(2 * cc + 4))
                    if cc >= 2:
                        act.wait_ge(s_used, nb + (2 * cc + 1 + RING + 1))
                        if cc >= 3:
                            act.wait_ge(s_qt, l * 5 + (cc - 2))
                        b = 2 * (cc % 2)
                        slot = {3: 0, 4: 1, 5: 0}.get(cc)
                        for t in range(TILES):
                            src = ps[:, b + t, :]
                            if cc == 2:
                                ins = nc.scalar.activation(v_sb[:, t, 0:512], src, ACT.Copy)
                            elif cc == 3:
                                ins = nc.scalar.activation(q_stage[:, slot, t, :], src, ACT.Copy)
                            elif cc == 4:
                                nc.scalar.activation(v_sb[:, t, 512:768], src[:, 0:256], ACT.Copy)
                                ins = nc.scalar.activation(q_stage[:, slot, t, 0:256], src[:, 256:512], ACT.Copy)
                            else:
                                nc.scalar.activation(v_sb[:, t, 768:1024], src[:, 256:512], ACT.Copy)
                                ins = nc.scalar.activation(q_stage[:, slot, t, 0:256], src[:, 0:256], ACT.Copy)
                        ins.then_inc(s_qev, 1)
                    if cc in (1, 2, 4, 5):
                        qk_copy({1: 0, 2: 1, 4: 2, 5: 3}[cc])
                split(nb, qb, 15)
                split(nb, qb, 16)
                act.wait_ge(s_fx, l + 1)
                link(nc.scalar.activation(f_l, f_x, ACT.Abs))
                link(nc.scalar.activation(f_l, f_l, ACT.Exp, scale=-1.0))
                nc.scalar.activation(f_l, f_l, ACT.Ln, bias=1.0).then_inc(s_fln, 1)
                qk_copy(4)

                def gates_copy(g):
                    act.wait_ge(s_used, nb + (U_GATE + 2 * g + 1 + RING + 1))
                    for t in range(TILES):
                        ins = nc.scalar.activation(gates[:, t, g // 2, 512 * (g % 2):512 * (g % 2) + 512],
                                                   ps[:, t, :], ACT.Copy)
                    ins.then_inc(s_gl, 1)

                def exps_first(g):
                    kind, t = GROUPS[g]
                    m, keys = groups_of(kind, t)
                    if kind == "sb":
                        act.wait_ge(s_sc, l * 6 + (g + 1))
                        if g >= 2:
                            act.wait_ge(s_wt, l * ROUNDS + ROUNDS_BEFORE[g - 1])
                        buf = prob(g)[:, 0:m * keys]
                        link(nc.scalar.activation(buf.rearrange("p (a n) -> p a n", a=2), scores_of(g), ACT.Abs))
                        link(nc.scalar.activation(buf, buf, ACT.Exp, scale=-1.0))
                        nc.scalar.activation(buf, buf, ACT.Ln, bias=1.0).then_inc(s_sbl, 1)

                def exps(g):
                    kind, t = GROUPS[g]
                    m, keys = groups_of(kind, t)
                    act.wait_ge(s_ei, l * 6 + (g + 1))
                    buf = prob(g)
                    if kind == "sb":
                        nc.scalar.activation(buf[:, 0:m * keys], sb_tmp[:, 0:m * keys], ACT.Exp).then_inc(s_ex, 1)
                        return
                    for j in range(m):
                        ins = nc.scalar.activation(buf[:, j * keys:(j + 1) * keys], buf[:, j * keys:(j + 1) * keys],
                                                   ACT.Exp, bias=negmax[:, j:j + 1], accum_out=psum_s[:, j:j + 1])
                    ins.then_inc(s_ex, 1)

                def heads_copy(g):
                    kind, t = GROUPS[g]
                    for r in range(t + 1):
                        n = ROUNDS_BEFORE[g] + r + 1
                        act.wait_ge(s_wt, l * ROUNDS + n)
                        nc.scalar.activation(wT[:, r, :, :], ps[:, 6 + r, :].rearrange("p (h n) -> p h n", h=4),
                                             ACT.Copy).then_inc(s_wte, 1)
                    width = 512 if kind == "diff" else 256
                    act.wait_ge(s_pv, l * 6 + (g + 1))
                    nc.scalar.activation(cat[:, t, CAT_OFF[kind]:CAT_OFF[kind] + width], ps[:, 6, 0:width],
                                         ACT.Copy).then_inc(s_pve, 1)

                for g in range(6):
                    exps_first(g)
                    split(nb, qb, U_GATE + 2 * g + 3, mix_words(U_GATE + 2 * g + 3))
                    if g == 0:
                        act.wait_ge(s_F, l + 1)
                        nc.scalar.activation(f_row[0:NF, :], ps[0:NF, 6, 0:SEQ], ACT.Copy).then_inc(s_Fr, 1)
                    exps(g)
                    split(nb, qb, U_GATE + 2 * g + 4, mix_words(U_GATE + 2 * g + 4))
                    gates_copy(g)
                    if g >= 1:
                        heads_copy(g - 1)
                        if GROUPS[g - 1][0] == "diff":
                            rsqrt_seed(l * 4 + (1 if g - 1 == 0 else 2), 4)
                heads_copy(5)
                transposed_hi(l * 4 + 1, act_hi)
                for cc in range(2):
                    for t in range(TILES):
                        part = gates[:, t, :, 512 * cc:512 * cc + 512]
                        nc.scalar.activation(part, part, ACT.Sigmoid).then_inc(s_sg, 1)
                    for b in range(3):
                        split(nb, qb, U_UP + 3 * cc + b + 3, mix_words(U_UP + 3 * cc + b + 3))
                transposed_hi(l * 4 + 2, mrg_hi)
                for k in range(4):
                    split(nb, qb, U_OUT + k + 3)
                rsqrt_seed(l * 4 + 3, TILES)
                transposed_hi(l * 4 + 3, act_hi)

                act.wait_ge(s_rd, l + 1)
                nc.scalar.activation(ee, dd, ACT.Exp).then_inc(s_re, 1)

                def gathered_hi(index):
                    for b in range(2):
                        act.wait_ge(s_ga, index * 2 + (b + 1))
                        nc.scalar.activation(x_hi[:, 4 * b:4 * b + 4, :],
                                             ps[:, 1 + 2 * b, :].rearrange("p (k n) -> p k n", k=4),
                                             ACT.Copy).then_inc(s_xh, 1)

                gathered_hi(l * (DENSE_ITEMS + 1))
                hold(act, s_tab, l + 1)
                n_items = act.value_load(itab[0:1, 0:1], min_val=2, max_val=ITEMS)
                with act.Fori(0, n_items) as i:
                    item = l * DENSE_ITEMS + i
                    inb = l * LAYER_UNITS + i * ITEM_UNITS + MIX_UNITS
                    iqb = l * (LAYER_UNITS // RING) + i * (ITEM_UNITS // RING) + MIX_UNITS // RING
                    it7 = item * FC

                    def sigmoid(ub, u_done, f_par):
                        act.wait_ge(s_used, ub + (u_done + RING + 1))
                        nc.scalar.activation(sig[:], ps[:, f_par, :], ACT.Sigmoid).then_inc(s_sig, 1)

                    def hidden_hi(count):
                        act.wait_ge(s_tr, count)
                        nc.scalar.activation(hid_hi[:], ps[:, 6, :].rearrange("p (k n) -> p k n", k=4),
                                             ACT.Copy).then_inc(s_th, 1)

                    split(inb, iqb, 3)
                    split(inb, iqb, 4)
                    sigmoid(inb, 1, 0)
                    split(inb, iqb, 5)
                    split(inb, iqb, 6)
                    act.wait_ge(s_sT, item + 1)
                    nc.scalar.activation(scat[:], ps[:, 3, 0:TILES * P].rearrange("p (t n) -> p t n", t=TILES),
                                         ACT.Copy).then_inc(s_sTe, 1)
                    with act.Fori(0, FC // 2) as j:
                        jnb, jqb = inb + j * 12, iqb + j * 2
                        for u in range(2):
                            k0 = 4 + 6 * u
                            done = it7 + j * 2 + u
                            split(jnb, jqb, k0 + 3)
                            split(jnb, jqb, k0 + 4)
                            hidden_hi(done + 1)
                            act.wait_ge(s_gs, done + 1)
                            sigmoid(jnb, k0 + 1, (u + 1) % 2)
                            split(jnb, jqb, k0 + 5)
                            split(jnb, jqb, k0 + 6)
                            split(jnb, jqb, k0 + 7)
                            split(jnb, jqb, k0 + 8)
                    hidden_hi(it7 + FC)
                    gathered_hi(item + l + 1)
                    split(inb, iqb, ITEM_UNITS + 1)
                    split(inb, iqb, ITEM_UNITS + 2)
                    act.wait_ge(s_used, inb + (ITEM_UNITS - 1 + RING + 1))
                    nc.scalar.activation(d_sb[:, 0:512], ps[:, 4, :], ACT.Copy).then_inc(s_dA, 1)
                rsqrt_seed(l * 4 + 4, TILES)
                transposed_hi(l * 4 + 4, act_hi)
                assert link_count[1] == ACT_LAYER

        @block.vector
        def _(dve):
            link_count = [0, 0]

            def link(ins):
                link_count[1] += 1
                ins.then_inc(s_dch, 1)
                dve.wait_ge(s_dch, link_count[0] + link_count[1])

            def split(nb, k, n=2048):
                dve.wait_ge(s_hi, nb + (k + 1))
                nc.vector.tensor_tensor(w_lo[:, k % RING, 0:n], raw[:, k % RING, 0:n],
                                        w_hi[:, k % HRING, 0:n].bitcast(F32), ALU.subtract).then_inc(s_lo, 1)

            def refine(index, n, out_ap):
                dve.wait_ge(s_rr, index + 1)
                link(nc.vector.tensor_tensor(rn[:, 0:n], rr[:, 0:n], rr[:, 0:n], ALU.mult))
                link(nc.vector.tensor_tensor(rn[:, 0:n], rn[:, 0:n], rv[:, 0:n], ALU.mult))
                link(nc.vector.tensor_scalar(rn[:, 0:n], rn[:, 0:n], -0.5, 1.5, ALU.mult, ALU.add))
                link(nc.vector.tensor_tensor(out_ap, rn[:, 0:n], rr[:, 0:n], ALU.mult))

            def normalise(index, ln_index):
                for t in range(TILES):
                    for b in range(2):
                        link(nc.vector.bn_stats(bst[:, b, :], h[:, t, 512 * b:512 * b + 512]))
                    dve.sem_inc(s_passed, 1)
                    link(nc.vector.bn_aggr(mv[:, t, :], bst.rearrange("p c m -> p (c m)")))
                nc.vector.tensor_scalar(rv[:, 0:TILES], mv[:, :, 1], 1e-5, None, ALU.add).then_inc(s_rv, 1)
                refine(index, TILES, rn[:, 0:TILES])
                dve.wait_ge(s_gb, (ln_index + 1) * 16)
                for t in range(TILES):
                    link(nc.vector.tensor_scalar(h[:, t, :], h[:, t, :], mv[:, t, 0:1], rn[:, t:t + 1],
                                                 ALU.subtract, ALU.mult))
                    link(nc.vector.tensor_tensor(h[:, t, :], h[:, t, :], ln_gb[:, 0, :], ALU.mult))
                    ins = nc.vector.tensor_tensor(h[:, t, :], h[:, t, :], ln_gb[:, 1, :], ALU.add)
                    ins.then_inc(s_h, 1)
                dve.wait_ge(s_h, (ln_index + 1) * TILES)
                dve.sem_inc(s_lnd, 1)

            def transposed_lo(job, hi, lo):
                for step in range(4):
                    t, half = step // 2, step % 2
                    dve.wait_ge(s_tph, job * 4 + (step + 1))
                    part = (slice(None), slice(4 * half, 4 * half + 4), slice(t * P, t * P + P))
                    nc.vector.tensor_tensor(lo[part], ps[:, 2 + step, :].rearrange("p (k n) -> p k n", k=4),
                                            hi[part].bitcast(F32), ALU.subtract).then_inc(s_tpl, 1)

            dve.sem_inc(s_dV, 1)
            for k in range(HRING):
                split(0, k)
            dve.wait_ge(s_cst, 16)
            dve.wait_ge(s_par, 16 * PARAM_LOADS)
            for l in range(DEPTH):
                for m in range(2):
                    link(nc.vector.tensor_tensor(rt[:, 0:HD], lamq[:, l, 2 * m, :], lamq[:, l, 2 * m + 1, :], ALU.mult))
                    link(nc.vector.reduce_sum(lam_s[:, 2 * l + m:2 * l + m + 1], rt[:, 0:HD], AX))
            dve.sem_inc(s_lam, 1)
            dve.wait_ge(s_lame, 1)
            for l in range(DEPTH):
                link(nc.vector.tensor_tensor(lam[:, l:l + 1], lam_e[:, 2 * l:2 * l + 1], lam_e[:, 2 * l + 1:2 * l + 2], ALU.subtract))
                a = COLS["layer"][0] + 4 * l
                link(nc.vector.tensor_tensor(lam[:, l:l + 1], lam[:, l:l + 1], cst[:, a:a + 1], ALU.add))
            dve.wait_ge(s_x, 16)
            normalise(0, 0)
            transposed_lo(0, act_hi, act_lo)
            before_loop = link_count[1]

            with dve.Fori(0, DEPTH) as l:
                nb = l * LAYER_UNITS
                link_count[0], link_count[1] = l * DVE_LAYER + before_loop, 0
                a = COLS["layer"][0]
                link(nc.vector.tensor_copy(lay, cst[:, a:a + 4 * DEPTH].rearrange("p (l m) -> p l m", l=DEPTH)[:, bass.ds(l, 1), :]
                                           .rearrange("p a m -> p (a m)")))
                link(nc.vector.tensor_copy(bf, bf2[:, bass.ds(l, 1), :].rearrange("p a m -> p (a m)")))
                link(nc.vector.tensor_scalar(neg_lam, lam[:, bass.ds(l, 1)], -1.0, None, ALU.mult))
                link(nc.vector.tensor_scalar(diffg, diffg2[:, bass.ds(l, 1), :].rearrange("p a m -> p (a m)"),
                                             lay[:, 1:2], None, ALU.mult))

                def rope(cc):
                    dve.wait_ge(s_used, nb + (2 * cc + 1 + RING + 1))
                    for t in range(TILES):
                        src = ps[:, 2 * cc + t, :].rearrange("p (m h d) -> p m h d", m=8, h=2)
                        dst = q_stage[:, cc, t, :].rearrange("p (m h d) -> p m h d", m=8, h=2)
                        swp = sb_tmp[:, 512 * (t % 2):512 * (t % 2) + 512].rearrange("p (m h d) -> p m h d", m=8, h=2)

                        def table(name, hh):
                            a = COLS[name][0] + HD * t + HD // 2 * hh
                            return cst[:, a:a + HD // 2].unsqueeze(1).to_broadcast([P, 8, HD // 2])

                        for hh in range(2):
                            nc.vector.tensor_tensor(dst[:, :, hh, :], src[:, :, hh, :], table("cos", hh), ALU.mult)
                            ins = nc.vector.tensor_tensor(swp[:, :, hh, :], src[:, :, 1 - hh, :], table("sin", hh), ALU.mult)
                        link(ins)
                        nc.vector.tensor_tensor(q_stage[:, cc, t, :], q_stage[:, cc, t, :],
                                                sb_tmp[:, 512 * (t % 2):512 * (t % 2) + 512], ALU.add).then_inc(s_rope, 1)

                for cc in range(6):
                    split(nb, 2 * cc + 3, mix_words(2 * cc + 3))
                    split(nb, 2 * cc + 4, mix_words(2 * cc + 4))
                    if cc < 2:
                        rope(cc)
                split(nb, 15)
                split(nb, 16)
                dve.wait_ge(s_used, nb + (U_F + 1 + RING + 1))
                for t in range(TILES):
                    ins = nc.vector.tensor_tensor(f_x[:, NF * t:NF * t + NF], ps[:, 6 + t, 0:NF], bf, ALU.add)
                ins.then_inc(s_fx, 1)
                dve.wait_ge(s_fln, l + 1)
                nc.vector.scalar_tensor_tensor(lf.rearrange("p t f -> p (t f)"), f_x, 0.0, f_l, ALU.min, ALU.subtract).then_inc(s_lf, 1)

                def group_first(g):
                    kind, t = GROUPS[g]
                    m, keys = groups_of(kind, t)
                    buf = prob(g)[:, 0:m * keys]
                    b3 = buf.rearrange("p (m k) -> p m k", m=m)
                    mask = {"diff": c(f"mdiff{t}"), "fox": c(f"mfox{t}"), "sb": c(f"msb{t}")}[kind]
                    mask3 = mask.unsqueeze(1).to_broadcast([P, m, keys])
                    z = scores_of(g)

                    def halves(a):
                        return a.rearrange("p (a n) -> p a n", a=2)

                    def score(j):
                        pos = place_of(g, j)
                        o = pos % (m // 2) * keys
                        return z[:, pos // (m // 2), o:o + keys]

                    dve.wait_ge(s_sc, l * 6 + (g + 1))
                    if kind == "sb":
                        u = sb_tmp[:, 0:m * keys]
                        u3 = u.rearrange("p (m k) -> p m k", m=m)
                        dve.wait_ge(s_sbl, l * 2 + (1 if g == 1 else 2))
                        link(nc.vector.scalar_tensor_tensor(halves(u), z, 0.0, halves(buf), ALU.max, ALU.add))
                        link(nc.vector.scalar_tensor_tensor(u3, mask3, 0.0, u3, ALU.is_ge, ALU.mult))
                        for j in range(m):
                            ins = nc.vector.tensor_tensor_scan(b3[:, j, ::-1], u3[:, j, ::-1], u3[:, j, ::-1],
                                                               0.0, ALU.add, ALU.max)
                        link(ins)
                        ins = nc.vector.tensor_tensor(halves(u), z, halves(buf), ALU.subtract)
                        link(ins)
                        dve.sem_inc(s_scr, 1)
                        nc.vector.tensor_tensor(u3, u3, mask3, ALU.add).then_inc(s_ei, 1)
                        return
                    if g >= 2:
                        dve.wait_ge(s_wt, l * ROUNDS + ROUNDS_BEFORE[g - 1])
                    if kind == "diff":
                        ins = nc.vector.tensor_tensor(b3, z.rearrange("p a n -> p (a n)").rearrange("p (m k) -> p m k", m=m), mask3, ALU.add)
                    else:
                        if g == 2:
                            dve.wait_ge(s_Fc, l + 1)
                        for j in range(m):
                            ins = nc.vector.scalar_tensor_tensor(b3[:, place_of(g, j), :], score(j), f_col[:, t, j:j + 1],
                                                                 mask, ALU.add, ALU.add)
                    link(ins)
                    dve.sem_inc(s_scr, 1)
                    link(nc.vector.tensor_reduce(negmax[:, 0:m], b3, AX, ALU.max, negate=True))
                    dve.sem_inc(s_ei, 1)

                def group_last(g):
                    kind, t = GROUPS[g]
                    m, keys = groups_of(kind, t)
                    if kind == "sb":
                        return
                    b3 = prob(g)[:, 0:m * keys].rearrange("p (m k) -> p m k", m=m)
                    dve.wait_ge(s_ex, l * 6 + (g + 1))
                    link(nc.vector.reciprocal(rsum[:, 0:m], psum_s[:, 0:m]))
                    if kind == "diff":
                        link(nc.vector.tensor_scalar(rsum[:, 4:8], rsum[:, 4:8], neg_lam, None, ALU.mult))
                    ins = nc.vector.tensor_tensor(b3, b3, rsum[:, 0:m].unsqueeze(2).to_broadcast([P, m, keys]), ALU.mult)
                    if kind == "diff":
                        link(ins)
                        ins = nc.vector.tensor_tensor(b3[:, 0:4, :], b3[:, 0:4, :], b3[:, 4:8, :], ALU.add)
                    ins.then_inc(s_w, 1)

                def rms(g):
                    t = GROUPS[g][1]
                    index = l * 4 + (1 if g == 0 else 2)
                    o = cat[:, t, 0:512]
                    o3 = o.rearrange("p (h v) -> p h v", h=4)
                    dve.wait_ge(s_pve, l * 6 + (g + 1))
                    link(nc.vector.tensor_tensor(sq[:], o, o, ALU.mult))
                    link(nc.vector.tensor_reduce(rv[:, 0:4], sq[:].rearrange("p (h v) -> p h v", h=4), AX, ALU.add))
                    nc.vector.tensor_scalar(rv[:, 0:4], rv[:, 0:4], 1.0 / P, 1e-6, ALU.mult, ALU.add).then_inc(s_rv, 1)
                    refine(index, 4, rn[:, 0:4])
                    link(nc.vector.tensor_tensor(o3, o3, rn[:, 0:4].unsqueeze(2).to_broadcast([P, 4, P]), ALU.mult))
                    nc.vector.tensor_tensor(o3, o3, diffg.unsqueeze(1).to_broadcast([P, 4, P]), ALU.mult).then_inc(s_rms, 1)

                for g in range(6):
                    if g == 0:
                        group_first(g)
                        split(nb, U_GATE + 3)
                        dve.wait_ge(s_F, l + 1)
                        nc.vector.tensor_copy(f_col, ps[:, 7, 0:TILES * NF].rearrange("p (t f) -> p t f", t=TILES)).then_inc(s_Fc, 1)
                    else:
                        group_first(g)
                        split(nb, U_GATE + 2 * g + 3, mix_words(U_GATE + 2 * g + 3))
                    group_last(g)
                    split(nb, U_GATE + 2 * g + 4, mix_words(U_GATE + 2 * g + 4))
                    if g in (1, 4):
                        rms(g - 1)
                transposed_lo(l * 4 + 1, act_hi, act_lo)
                for cc in range(2):
                    def part(t, b):
                        return gates[:, t, b, 512 * cc:512 * cc + 512]
                    for b in range(3):
                        k = U_UP + 3 * cc + b
                        split(nb, k + 3, mix_words(k + 3))
                        dve.wait_ge(s_used, nb + (k + RING + 1))
                        for t in range(TILES):
                            dve.wait_ge(s_sg, l * 4 + (2 * cc + t + 1))
                            ins = nc.vector.tensor_tensor(part(t, b), part(t, b), ps[:, 2 * b + t, :], ALU.mult)
                        ins.then_inc(s_gm, 1)
                    dve.wait_ge(s_gm, l * 6 + (3 * cc + 3))
                    for t in range(TILES):
                        m = cat[:, t, 512 * cc:512 * cc + 512]
                        link(nc.vector.tensor_tensor(m, part(t, 0), part(t, 1), ALU.add))
                        nc.vector.tensor_tensor(m, m, part(t, 2), ALU.add).then_inc(s_mrg, 1)
                transposed_lo(l * 4 + 2, mrg_hi, mrg_lo)
                for k in range(4):
                    split(nb, U_OUT + k + 3)
                    if k % 2:
                        dve.wait_ge(s_used, nb + (U_OUT + k + RING + 1))
                        for t in range(TILES):
                            part_h = h[:, t, 256 * (k - 1):256 * (k - 1) + 512]
                            ins = nc.vector.scalar_tensor_tensor(part_h, part_h, ALPHA, ps[:, 3 * (k - 1) + t, :], ALU.mult, ALU.add)
                        link(ins)
                normalise(l * 4 + 3, l * 2 + 1)
                transposed_lo(l * 4 + 3, act_hi, act_lo)

                nc.vector.memset(d_sb[:], 0.0)
                nc.vector.memset(scat[:], 0.0)
                nc.vector.memset(cat[:], 0.0)
                nc.vector.memset(tab_rk, -1.0)
                nc.vector.memset(tab_cw, 0.0)
                link(nc.vector.memset(item_cw, 0.0))
                e16 = [P, TILES, N_EXP]

                def wide(a):
                    return a.to_broadcast(e16)

                def cols(name):
                    return c(name).unsqueeze(1).to_broadcast(e16)

                dve.wait_ge(s_lg, l + 1)
                for t in range(TILES):
                    ins = nc.vector.tensor_tensor(lg[:, t, :], ps[:, 6 + t, 0:N_EXP], b_rt, ALU.add)
                link(ins)

                def first_largest(logits, largest, onehot):
                    link(nc.vector.tensor_reduce(largest.rearrange("p t e -> p (t e)"), logits, AX, ALU.max))
                    link(nc.vector.tensor_tensor(eq, logits, wide(largest), ALU.is_equal))
                    link(nc.vector.tensor_tensor(eq, eq, cols("first"), ALU.mult))
                    link(nc.vector.tensor_reduce(fi.rearrange("p t e -> p (t e)"), eq, AX, ALU.min))
                    link(nc.vector.tensor_tensor(onehot, cols("first"), wide(fi), ALU.is_equal))

                first_largest(lg, m1, oh1)
                link(nc.vector.scalar_tensor_tensor(lg2, oh1, -3e38, lg, ALU.mult, ALU.add))
                first_largest(lg2, m2, oh2)
                nc.vector.tensor_tensor(sel, oh1, oh2, ALU.add).then_inc(s_sel, 1)
                nc.vector.tensor_tensor(dd, m2, m1, ALU.subtract).then_inc(s_rd, 1)
                dve.wait_ge(s_re, l + 1)
                link(nc.vector.tensor_scalar(w1, ee, 1.0, None, ALU.add))
                link(nc.vector.reciprocal(w1, w1))
                link(nc.vector.tensor_tensor(w2, w1, ee, ALU.mult))
                link(nc.vector.tensor_tensor(cwe, oh1, wide(w1), ALU.mult))
                link(nc.vector.tensor_tensor(eq, oh2, wide(w2), ALU.mult))
                link(nc.vector.tensor_tensor(cwe, cwe, eq, ALU.add))
                dve.wait_ge(s_rk, l + 1)
                link(nc.vector.tensor_tensor(rkm, ps[:, 6, 0:TILES * N_EXP].rearrange("p (t e) -> p t e", t=TILES), sel, ALU.mult))
                link(nc.vector.tensor_scalar(rkm, rkm, -1.0, None, ALU.add))
                link(nc.vector.tensor_scalar(ov, ps[:, 7, 0:N_EXP], float(P), None, ALU.is_gt))
                link(nc.vector.tensor_tensor_scan(inc, ov, ov, 0.0, ALU.add, ALU.max))
                link(nc.vector.tensor_tensor(exc, inc, ov, ALU.subtract))
                link(nc.vector.tensor_copy(tab_rk[:, :, 0:N_EXP], rkm))
                link(nc.vector.tensor_copy(tab_cw[:, :, 0:N_EXP], cwe))
                link(nc.vector.tensor_copy(ftab[:, 1:], c("expert")))
                for j in range(ITEMS - N_EXP):
                    link(nc.vector.scalar_tensor_tensor(osel, exc, float(j), ov, ALU.is_equal, ALU.mult))
                    oj = osel.unsqueeze(1).to_broadcast(e16)
                    col = slice(N_EXP + j, N_EXP + j + 1)
                    for table, values in ((tab_rk, rkm), (tab_cw, cwe)):
                        link(nc.vector.tensor_tensor(prod, values, oj, ALU.mult))
                        link(nc.vector.tensor_reduce(table[:, :, col].rearrange("p t i -> p (t i)"), prod, AX, ALU.add))
                    link(nc.vector.tensor_tensor(wrb, osel, c("iota8"), ALU.mult))
                    link(nc.vector.tensor_reduce(ftab[:, 1 + N_EXP + j:2 + N_EXP + j], wrb, AX, ALU.add))
                link(nc.vector.tensor_scalar(tab_rk[:, :, N_EXP:ITEMS], tab_rk[:, :, N_EXP:ITEMS], float(-P), None, ALU.add))
                link(nc.vector.tensor_scalar(ftab[:, 1 + N_EXP:1 + ITEMS], ftab[:, 1 + N_EXP:1 + ITEMS], 1.0, None, ALU.add))
                link(nc.vector.tensor_scalar(ftab[:, 0:1], inc[:, N_EXP - 1:N_EXP], float(N_EXP), None, ALU.add))
                link(nc.vector.tensor_scalar(ftab, ftab, lay[:, 2:3], None, ALU.mult))
                link(nc.vector.scalar_tensor_tensor(ftab[:, 0:1], lay[:, 3:4], float(DENSE_ITEMS), ftab[:, 0:1], ALU.mult, ALU.add))
                nc.vector.tensor_copy(itab[:, 0:ITEM_COLS + 1], ftab).then_inc(s_tab, 1)
                drk = c("drk").rearrange("p (t i) -> p t i", t=TILES)
                link(nc.vector.tensor_scalar(item_rk, tab_rk, lay[:, 2:3], None, ALU.mult))
                link(nc.vector.scalar_tensor_tensor(item_rk, drk, lay[:, 3:4], item_rk, ALU.mult, ALU.add))
                link(nc.vector.tensor_scalar(item_cw[:, :, 1:], tab_cw, lay[:, 2:3], None, ALU.mult))
                link(nc.vector.tensor_scalar(item_cw[:, :, 1:], item_cw[:, :, 1:], lay[:, 3:4], None, ALU.add))

                def gather_matrix(i):
                    for t in range(TILES):
                        ins = nc.vector.tensor_scalar(gath[:, t, :], iota, item_rk[:, t, bass.ds(i, 1)], None, ALU.is_equal)
                    ins.then_inc(s_S, 1)

                def gathered_lo(index):
                    for b in range(2):
                        dve.wait_ge(s_xh, index * 2 + (b + 1))
                        nc.vector.tensor_tensor(x_lo[:, 4 * b:4 * b + 4, :],
                                                ps[:, 1 + 2 * b, :].rearrange("p (k n) -> p k n", k=4),
                                                x_hi[:, 4 * b:4 * b + 4, :].bitcast(F32), ALU.subtract).then_inc(s_xl, 1)

                def add_item(index, i):
                    for q, bank in enumerate((4, 5, 7, 6)):
                        t, half = q // 2, q % 2
                        dve.wait_ge(s_cb, index * 4 + (q + 1))
                        part_y = cat[:, t, 512 * half:512 * half + 512]
                        nc.vector.scalar_tensor_tensor(part_y, ps[:, bank, :], item_cw[:, t, bass.ds(i, 1)], part_y,
                                                       ALU.mult, ALU.add).then_inc(s_ac, 1)

                gather_matrix(0)
                gathered_lo(l * (DENSE_ITEMS + 1))
                hold(dve, s_tab, l + 1)
                n_items = dve.value_load(itab[0:1, 0:1], min_val=2, max_val=ITEMS)
                with dve.Fori(0, n_items) as i:
                    item = l * DENSE_ITEMS + i
                    inb = l * LAYER_UNITS + i * ITEM_UNITS + MIX_UNITS
                    it7 = item * FC

                    def gate_silu(count, f_par):
                        dve.wait_ge(s_sig, count)
                        nc.vector.tensor_tensor(gsig[:], ps[:, f_par, :], sig[:], ALU.mult).then_inc(s_gs, 1)

                    def hidden(count, ub, u_done, f_par):
                        dve.wait_ge(s_used, ub + (u_done + RING + 1))
                        dve.wait_ge(s_gs, count)
                        nc.vector.tensor_tensor(hid[:], ps[:, 2 + f_par, :], gsig[:], ALU.mult).then_inc(s_hd, 1)

                    def hidden_lo(count):
                        dve.wait_ge(s_th, count)
                        nc.vector.tensor_tensor(hid_lo[:], ps[:, 6, :].rearrange("p (k n) -> p k n", k=4),
                                                hid_hi[:].bitcast(F32), ALU.subtract).then_inc(s_tl, 1)

                    split(inb, 3)
                    split(inb, 4)
                    gate_silu(it7 + 1, 0)
                    split(inb, 5)
                    hidden(it7 + 1, inb, 3, 0)
                    split(inb, 6)
                    add_item(item + l, i)
                    with dve.Fori(0, FC // 2) as j:
                        jnb = inb + j * 12
                        for u in range(2):
                            k0 = 4 + 6 * u
                            done = it7 + j * 2 + u
                            split(jnb, k0 + 3)
                            split(jnb, k0 + 4)
                            hidden_lo(done + 1)
                            gate_silu(done + 2, (u + 1) % 2)
                            split(jnb, k0 + 5)
                            split(jnb, k0 + 6)
                            hidden(done + 2, jnb, k0 + 3, (u + 1) % 2)
                            split(jnb, k0 + 7)
                            split(jnb, k0 + 8)
                    dve.wait_ge(s_sT, item + 1)
                    gather_matrix(i + 1)
                    hidden_lo(it7 + FC)
                    gathered_lo(item + l + 1)
                    split(inb, ITEM_UNITS + 1)
                    split(inb, ITEM_UNITS + 2)
                    dve.wait_ge(s_used, inb + (ITEM_UNITS - 1 + RING + 1))
                    nc.vector.tensor_copy(d_sb[:, 512:1024], ps[:, 5, :]).then_inc(s_dV, 1)
                last = l * DENSE_ITEMS + l + n_items
                add_item(last, n_items)
                dve.wait_ge(s_ac, last * 4 + 4)
                for t in range(TILES):
                    ins = nc.vector.scalar_tensor_tensor(h[:, t, :], h[:, t, :], ALPHA, cat[:, t, :], ALU.mult, ALU.add)
                link(ins)
                normalise(l * 4 + 4, l * 2 + 2)
                transposed_lo(l * 4 + 4, act_hi, act_lo)
                assert link_count[1] == DVE_LAYER, link_count

        @block.tensor
        def _(pe):
            def product(dst, xh, xl, wh, wl, start, stop):
                nc.tensor.matmul(dst, xh, wh, start=start, stop=False)
                nc.tensor.matmul(dst, xh, wl, start=False, stop=False)
                return nc.tensor.matmul(dst, xl, wh, start=False, stop=stop)

            def unit(nb, k, banks, kts, width, hi, lo, first, last):
                pe.wait_ge(s_lo, nb + (k + 1))
                for t, bank in enumerate(banks):
                    for j, kt in enumerate(kts):
                        ins = product(ps[:, bank, 0:width], hi[:, kt, t * P:t * P + P], lo[:, kt, t * P:t * P + P],
                                      w_hi[:, k % HRING, j * width:(j + 1) * width],
                                      w_lo[:, k % RING, j * width:(j + 1) * width],
                                      first and j == 0, last and j == len(kts) - 1)
                ins.then_inc(s_used, 1)

            def transposes(wait, src):
                for step in range(4):
                    t, half = step // 2, step % 2
                    wait(t, half)
                    for b in range(4):
                        o = 512 * half + P * b
                        ins = nc.tensor.transpose(ps[:, 2 + step, b * P:b * P + P], src[:, t, o:o + P], ident)
                    ins.then_inc(s_tp, 1)

            nc.tensor.sem_inc(s_used, RING)
            pe.wait_ge(s_cst, 16)
            pe.wait_ge(s_par, 16 * PARAM_LOADS)
            pe.wait_ge(s_zero, 1)
            transposes(lambda t, half: pe.wait_ge(s_h, t + 1), h)

            with pe.Fori(0, DEPTH) as l:
                nb = l * LAYER_UNITS

                def qk_transposes(j, wait_stage):
                    cc, slot, nblk = [(0, 0, 4), (1, 1, 4), (3, 0, 4), (4, 1, 2), (5, 0, 2)][j]
                    wait_stage()
                    if j:
                        pe.wait_ge(s_qte, l * 5 + j)
                    for t in range(TILES):
                        for b in range(nblk):
                            ins = nc.tensor.transpose(ps[:, 4 + t, b * P:b * P + P],
                                                      q_stage[:, slot, t, b * P:b * P + P], ident)
                    ins.then_inc(s_qt, 1)

                pe.wait_ge(s_tpl, l * 16 + 4)
                for cc in range(6):
                    if cc in (2, 3):
                        pe.wait_ge(s_rope, l * 4 + 2 * (cc - 1))
                    if cc in (4, 5):
                        pe.wait_ge(s_qev, l * 4 + (cc - 3))
                    b = 2 * (cc % 2)
                    for hk in range(2):
                        unit(nb, 2 * cc + hk, (b, b + 1), range(4 * hk, 4 * hk + 4), 512, act_hi, act_lo, hk == 0, hk == 1)
                    if cc == 1:
                        qk_transposes(0, lambda: pe.wait_ge(s_rope, l * 4 + 2))
                    if cc == 2:
                        qk_transposes(1, lambda: pe.wait_ge(s_rope, l * 4 + 4))
                    if cc == 4:
                        qk_transposes(2, lambda: pe.wait_ge(s_qev, l * 4 + 2))
                    if cc == 5:
                        qk_transposes(3, lambda: pe.wait_ge(s_qev, l * 4 + 3))
                for hk in range(2):
                    unit(nb, U_F + hk, (6, 7), range(4 * hk, 4 * hk + 4), NF, act_hi, act_lo, hk == 0, hk == 1)
                qk_transposes(4, lambda: pe.wait_ge(s_qev, l * 4 + 4))

                def scores(g):
                    kind, t = GROUPS[g]
                    m, keys = groups_of(kind, t)
                    if g == 0:
                        pe.wait_ge(s_qte, l * 5 + 5)
                    else:
                        pe.wait_ge(s_scr, l * 6 + FREED_BY[g])
                    if kind == "fox" and g == 2:
                        pe.wait_ge(s_Fr, l + 1)
                    z = scores_of(g)
                    for j in range(m):
                        blk, r = j // 2, HD * (j % 2)
                        pos = place_of(g, j)
                        o = pos % (m // 2) * keys
                        dst = z[:, pos // (m // 2), o:o + keys]
                        q = qkT[r:r + HD, Q_BLK[kind] + blk, t * P:t * P + P]
                        k = qkT[r:r + HD, K_BLK[kind] + blk, 0:keys]
                        ins = nc.tensor.matmul(dst, q, k, start=True, stop=kind != "fox")
                        if kind == "fox":
                            a = COLS["negsel"][0] + j * P
                            ins = nc.tensor.matmul(dst, cst[0:NF, a:a + P], f_row[0:NF, 0:keys], start=False, stop=True)
                    ins.then_inc(s_sc, 1)

                def heads(g):
                    kind, t = GROUPS[g]
                    m, keys = groups_of(kind, t)
                    buf = prob(g)
                    if kind == "sb":
                        pe.wait_ge(s_ex, l * 6 + (g + 1))
                    else:
                        pe.wait_ge(s_w, l * 4 + {0: 1, 2: 2, 3: 3, 5: 4}[g])
                    if g:
                        pe.wait_ge(s_pve, l * 6 + g)
                    else:
                        pe.wait_ge(s_Fr, l + 1)
                        pe.wait_ge(s_Fc, l + 1)
                    for r in range(t + 1):
                        for hh in range(4):
                            o = (hh if kind == "diff" else place_of(g, hh)) * keys + r * P
                            ins = nc.tensor.transpose(ps[:, 6 + r, hh * P:hh * P + P], buf[:, o:o + P], ident)
                        ins.then_inc(s_wt, 1)
                    pe.wait_ge(s_wte, l * ROUNDS + (ROUNDS_BEFORE[g] + t + 1))
                    width = P if kind == "diff" else HD
                    for hh in range(4):
                        for r in range(t + 1):
                            v0 = CAT_OFF[kind] + hh * width
                            ins = nc.tensor.matmul(ps[:, 6, hh * width:(hh + 1) * width], wT[:, r, hh, :],
                                                   v_sb[:, r, v0:v0 + width], start=(r == 0), stop=(r == t))
                    ins.then_inc(s_pv, 1)

                scores(0)
                for g in range(6):
                    if g:
                        pe.wait_ge(s_gl, l * 6 + g)
                    for hk in range(2):
                        unit(nb, U_GATE + 2 * g + hk, (0, 1), range(4 * hk, 4 * hk + 4), 512, act_hi, act_lo, hk == 0, hk == 1)
                    if g == 0:
                        pe.wait_ge(s_lf, l + 1)
                        for k in range(TILES):
                            nc.tensor.matmul(ps[0:NF, 6, 0:SEQ], lf[:, k, :], tri[:, k, :], start=(k == 0), stop=(k == TILES - 1))
                        nc.tensor.matmul(ps[:, 7, 0:NF], tri[:, 0, 0:P], lf[:, 0, :], start=True, stop=True)
                        for k in range(TILES):
                            ins = nc.tensor.matmul(ps[:, 7, NF:2 * NF], tri[:, k, P:2 * P], lf[:, k, :],
                                                   start=(k == 0), stop=(k == TILES - 1))
                        ins.then_inc(s_F, 1)
                    if g < 5:
                        scores(g + 1)
                    if g:
                        heads(g - 1)
                heads(5)

                def wait_heads(t, half):
                    pe.wait_ge(s_pve, l * 6 + 6)
                    pe.wait_ge(s_rms, l * 2 + 2)

                transposes(wait_heads, cat)
                pe.wait_ge(s_tpl, l * 16 + 8)
                pe.wait_ge(s_gl, l * 6 + 6)
                for cc in range(2):
                    for b in range(3):
                        if cc:
                            pe.wait_ge(s_gm, l * 6 + (b + 1))
                        k0, n = ((0, 4), (4, 2), (6, 2))[b]
                        unit(nb, U_UP + 3 * cc + b, (2 * b, 2 * b + 1), range(k0, k0 + n), 512, act_hi, act_lo, True, True)
                transposes(lambda t, half: pe.wait_ge(s_mrg, l * 4 + 4), cat)
                pe.wait_ge(s_tpl, l * 16 + 12)
                for cc in range(2):
                    for hk in range(2):
                        unit(nb, U_OUT + 2 * cc + hk, (6 * cc, 6 * cc + 1), range(4 * hk, 4 * hk + 4), 512, mrg_hi, mrg_lo, hk == 0, hk == 1)
                transposes(lambda t, half: pe.wait_ge(s_h, l * 4 + (TILES + t + 1)), h)

                pe.wait_ge(s_tpl, l * 16 + 16)
                for t in range(TILES):
                    n = 0
                    for part in (act_hi, act_lo):
                        for kt in range(KT):
                            ins = nc.tensor.matmul(ps[:, 6 + t, 0:N_EXP], part[:, kt, t * P:t * P + P].bitcast(F32),
                                                   w_rt[:, kt, :], start=(n == 0), stop=(n == 2 * KT - 1))
                            n += 1
                ins.then_inc(s_lg, 1)
                pe.wait_ge(s_sel, l + 1)
                nc.tensor.matmul(ps[:, 6, 0:N_EXP], tri[:, 0, 0:P], sel[:, 0, :], start=True, stop=True)
                for k in range(TILES):
                    nc.tensor.matmul(ps[:, 6, N_EXP:2 * N_EXP], tri[:, k, P:2 * P], sel[:, k, :], start=(k == 0), stop=(k == TILES - 1))
                for k in range(TILES):
                    ins = nc.tensor.matmul(ps[:, 7, 0:N_EXP], tri[:, 0, P:2 * P], sel[:, k, :], start=(k == 0), stop=(k == TILES - 1))
                ins.then_inc(s_rk, 1)

                def gather(index):
                    pe.wait_ge(s_S, index + 1)
                    for b in range(2):
                        for j in range(4):
                            o = (4 * b + j) * P
                            for t in range(TILES):
                                ins = nc.tensor.matmul(ps[:, 1 + 2 * b, j * P:j * P + P], h[:, t, o:o + P], gath[:, t, :],
                                                       start=(t == 0), stop=(t == TILES - 1))
                        ins.then_inc(s_ga, 1)

                def scatter(index, item_count):
                    pe.wait_ge(s_dA, item_count + 1)
                    pe.wait_ge(s_dV, item_count + 1)
                    pe.wait_ge(s_sTe, item_count + 1)
                    for q, bank in enumerate((4, 5, 7, 6)):
                        t, half = q // 2, q % 2
                        nc.tensor.matmul(ps[:, bank, :], scat[:, t, :], d_sb[:, 512 * half:512 * half + 512],
                                         start=True, stop=True).then_inc(s_cb, 1)

                gather(l * (DENSE_ITEMS + 1))
                hold(pe, s_tab, l + 1)
                n_items = pe.value_load(itab[0:1, 0:1], min_val=2, max_val=ITEMS)
                with pe.Fori(0, n_items) as i:
                    item = l * DENSE_ITEMS + i
                    inb = l * LAYER_UNITS + i * ITEM_UNITS + MIX_UNITS
                    it7 = item * FC
                    sc_index = item + l

                    def proj(ub, k, bank):
                        for hk in range(2):
                            unit(ub, k + hk, (bank,), range(4 * hk, 4 * hk + 4), 512, x_hi, x_lo, hk == 0, hk == 1)

                    def turn_hidden(count):
                        pe.wait_ge(s_hd, count)
                        for b in range(4):
                            ins = nc.tensor.transpose(ps[:, 6, b * P:b * P + P], hid[:, b * P:b * P + P], ident)
                        ins.then_inc(s_tr, 1)

                    def down(ub, k, count, last):
                        pe.wait_ge(s_tl, count)
                        for hk in range(2):
                            pe.wait_ge(s_lo, ub + (k + hk + 1))
                            for j in range(2):
                                for half in range(2):
                                    o = 1024 * j + 512 * half
                                    ins = product(ps[:, 4 + half, :], hid_hi[:, 2 * hk + j, :], hid_lo[:, 2 * hk + j, :],
                                                  w_hi[:, (k + hk) % HRING, o:o + 512], w_lo[:, (k + hk) % RING, o:o + 512],
                                                  False, last and hk == 1 and j == 1)
                            ins.then_inc(s_used, 1)

                    pe.wait_ge(s_xl, (item + l) * 2 + 2)
                    proj(inb, 0, 0)
                    proj(inb, 2, 2)
                    scatter(sc_index, item)
                    for t in range(TILES):
                        ins = nc.tensor.transpose(ps[:, 3, t * P:t * P + P], gath[:, t, :], ident)
                    ins.then_inc(s_sT, 1)
                    pe.wait_ge(s_ac, sc_index * 4 + 2)
                    for half in range(2):
                        nc.tensor.matmul(ps[:, 4 + half, :], zero_w[:], x_hi[:, 0:4, :].rearrange("p k n -> p (k n)"), start=True, stop=False)
                    with pe.Fori(0, FC // 2) as j:
                        jnb = inb + j * 12
                        for u in range(2):
                            k0 = 4 + 6 * u
                            done = it7 + j * 2 + u
                            proj(jnb, k0, (u + 1) % 2)
                            if u == 0:
                                pe.wait_ge(s_sTe, item + 2)
                                pe.wait_ge(s_ac, sc_index * 4 + 4)
                            turn_hidden(done + 1)
                            proj(jnb, k0 + 2, 2 + (u + 1) % 2)
                            down(jnb, k0 + 4, done + 1, False)
                    turn_hidden(it7 + FC)
                    gather(item + l + 1)
                    down(inb, 4 + 6 * (FC - 1), it7 + FC, True)
                scatter(l * DENSE_ITEMS + l + n_items, l * DENSE_ITEMS + n_items)
                transposes(lambda t, half: pe.wait_ge(s_h, l * 4 + (2 * TILES + t + 1)), h)


def kernel(**inputs):
    import numpy as _np
    import concourse.bacc as _bacc
    from concourse import mybir as _mybir
    from concourse.bass_utils import run_bass_kernel_spmd as _run

    a = {name: _np.asarray(value) for name, value in inputs.items()}
    sent = {
        "x": a["x"],
        "consts": constants(),
        "ln_in": _np.stack([a["ln_in_g"], a["ln_in_b"]]),
        "w_in": a["w_in"],
        "b_forget": a["b_forget"],
        "lam_qk": _np.stack([a["lam_q1"], a["lam_k1"], a["lam_q2"], a["lam_k2"]], axis=1),
        "diff_g": a["diff_norm_g"],
        "w_up_diff": a["w_up_diff"],
        "w_up_sb": a["w_up_sb"],
        "w_up_fox": a["w_up_fox"],
        "w_out": a["w_out"],
        "ln_mix": _np.stack([a["ln_mix_g"], a["ln_mix_b"]], axis=1),
        "ln_ffn": _np.stack([a["ln_ffn_g"], a["ln_ffn_b"]], axis=1),
        "w_router": a["w_router"],
        "b_router": a["b_router"],
        "w_gate": _np.concatenate([a["w_gate_dense"], a["w_gate_moe"][0]]),
        "w_up": _np.concatenate([a["w_up_dense"], a["w_up_moe"][0]]),
        "w_down": _np.concatenate([a["w_down_dense"], a["w_down_moe"][0]]),
    }
    nc = _bacc.Bacc("TRN2", target_bir_lowering=False, num_devices=1)
    arrays, args = {}, []
    for name, value in sent.items():
        value = _np.ascontiguousarray(value)
        arrays[f"in_{name}"] = value
        args.append(nc.dram_tensor(f"in_{name}", value.shape, _mybir.dt.from_np(value.dtype), kind="ExternalInput").ap())
    args.append(nc.dram_tensor("out_h", (1, SEQ, D), F32, kind="ExternalOutput").ap())
    build(nc, *args)
    r = _run(nc, [arrays], core_ids=[0])
    return r.results[0]["out_h"]
```

```python
import math
from contextlib import ExitStack

import numpy as np

import concourse.bass as bass
from concourse import mybir

F32 = mybir.dt.float32
F32R = mybir.dt.float32r
I32 = mybir.dt.int32
ALU = mybir.AluOpType
ACT = mybir.ActivationFunctionType
AX = mybir.AxisListType.X

P = 128
D = 1024
SEQ = 256
DEPTH = 2
TILES = SEQ // P
KT = D // P
CHUNK = 64
HD = 64
N_EXP = 8
D_FF = 3584
FC = D_FF // 512
ALPHA = (2 * DEPTH) ** 0.25
QKV = 3072
NF = 4
NEG = -1e30
ITEMS = N_EXP + SEQ * 2 // (P + 1)
ITEM_COLS = ITEMS + 1

RING, HRING = 6, 3
MIX_UNITS, ITEM_UNITS = 36, 6 * FC
DENSE_ITEMS = TILES
LAYER_UNITS = MIX_UNITS + DENSE_ITEMS * ITEM_UNITS
U_F, U_GATE, U_UP, U_OUT = 12, 14, 26, 32

GROUPS = [("diff", 1), ("sb", 1), ("fox", 1), ("diff", 0), ("sb", 0), ("fox", 0)]
BANK = [2, 2, 4, 2, 4, 2]
Q_BLK = {"diff": 0, "sb": 8, "fox": 12}
K_BLK = {"diff": 4, "sb": 10, "fox": 14}
CAT_OFF = {"diff": 0, "sb": 512, "fox": 768}
FREED_BY = [0, 1, 1, 2, 3, 4]
ROUNDS_BEFORE = [0, 2, 4, 6, 7, 8]
ROUNDS = 9
JOB = [(0, 0, 2), (0, 1, 3), (1, 0, 4), (1, 1, 5)]
HEADS_JOB = [(1, 0, 4), (1, 1, 5), (0, 0, 2), (0, 1, 3)]
MERGED_JOB = [(0, 0, 6), (1, 0, 7), (0, 1, 4), (1, 1, 5)]
SCATTER_BANKS = (1, 7, 3, 6)

COLS = {}
N_CONST = 0
for _name, _n in (("ident", P), ("tri", TILES * SEQ), ("iota", P), ("mfox1", 256), ("mfox0", 128),
                  ("mdiff1", 256), ("mdiff0", 128), ("msb1", 256), ("msb0", 128),
                  ("cos", TILES * HD), ("sin", TILES * HD), ("negsel", NF * P),
                  ("drk", TILES * ITEM_COLS), ("layer", DEPTH * 4), ("iota8", N_EXP),
                  ("first", N_EXP), ("expert", ITEM_COLS)):
    COLS[_name] = (N_CONST, N_CONST + _n)
    N_CONST += _n
PARAM_LOADS = 5


def mix_words(k):
    if U_F <= k < U_GATE:
        return 4 * NF
    return 1024 if U_UP <= k < U_OUT and (k - U_UP) % 3 else 2048


def constants():
    c = np.zeros((P, N_CONST), np.float32)

    def put(name, value):
        a, b = COLS[name]
        c[:, a:b] = np.broadcast_to(value, (P, b - a))

    p = np.arange(P)
    s = np.arange(SEQ)
    put("ident", np.eye(P))
    put("tri", np.concatenate([(p[:, None] + P * k <= s[None, :]) for k in range(TILES)], 1))
    put("iota", p[None, :])
    for t, n in ((1, 256), (0, 128)):
        q = p[:, None] + P * t
        k = np.arange(n)[None, :]
        put(f"mfox{t}", np.where(k <= q, 0.0, NEG))
        put(f"mdiff{t}", np.where(k // CHUNK <= q // CHUNK, 0.0, NEG))
        put(f"msb{t}", np.where(k < q, 0.0, NEG))
    half = HD // 2
    inv = (np.float32(10000.0) ** (-np.arange(half, dtype=np.float32) / np.float32(half))).astype(np.float32)
    ang = (s.astype(np.float32)[:, None] * inv[None, :]).astype(np.float32)
    cos, sin = np.cos(ang), np.sin(ang)
    put("cos", np.concatenate([np.tile(cos[P * t:P * t + P], (1, 2)) for t in range(TILES)], 1))
    put("sin", np.concatenate([np.concatenate([-sin[P * t:P * t + P], sin[P * t:P * t + P]], 1) for t in range(TILES)], 1))
    put("negsel", np.repeat(-np.eye(P, NF), P, axis=1))
    drk = np.full((P, TILES, ITEM_COLS), -1.0)
    for t in range(TILES):
        drk[:, t, t] = p
    put("drk", drk.reshape(P, -1))
    lam = [0.8 - 0.6 * math.exp(-0.3 * l) for l in range(DEPTH)]
    put("layer", np.array([[lam[l], 1.0 - lam[l], l % 2, 1 - l % 2] for l in range(DEPTH)]).reshape(1, -1))
    put("iota8", np.arange(N_EXP)[None, :])
    put("first", np.arange(N_EXP)[None, :] - 99.0)
    put("expert", np.array([1.0 + i if i < N_EXP else 0.0 for i in range(ITEM_COLS)])[None, :])
    return c


def mixer_stream(w_in, w_up_diff, w_up_sb, w_up_fox, w_out):
    stream = np.zeros((DEPTH, MIX_UNITS, P, 2048), w_in.dtype)

    def put(k, w, r0, r1, c0, c1):
        part = w[:, r0:r1, c0:c1].reshape(DEPTH, -1, P, c1 - c0).transpose(0, 2, 1, 3)
        stream[:, k, :, 0:mix_words(k)] = part.reshape(DEPTH, P, -1)

    for hk in range(2):
        r = 512 * hk
        for cc in range(6):
            put(2 * cc + hk, w_in, r, r + 512, 512 * cc, 512 * cc + 512)
            put(U_GATE + 2 * cc + hk, w_in, r, r + 512, QKV + NF + 512 * cc, QKV + NF + 512 * cc + 512)
        put(U_F + hk, w_in, r, r + 512, QKV, QKV + NF)
        for cc in range(2):
            put(U_OUT + 2 * hk + cc, w_out, r, r + 512, 512 * cc, 512 * cc + 512)
    for cc in range(2):
        for b, w in enumerate((w_up_diff, w_up_sb, w_up_fox)):
            put(U_UP + 3 * cc + b, w, 0, w.shape[1], 512 * cc, 512 * cc + 512)
    return stream


def item_stream(w_gate, w_up, w_down):
    n = w_gate.shape[0]
    stream = np.empty((n, ITEM_UNITS, P, 2048), w_gate.dtype)
    for f in range(FC):
        k = 6 * f - 2 if f else 0
        for j, w in enumerate((w_gate, w_up)):
            part = w[:, :, 512 * f:512 * f + 512].reshape(n, 2, 4, P, 512).transpose(0, 1, 3, 2, 4)
            stream[:, k + 2 * j:k + 2 * j + 2] = part.reshape(n, 2, P, 2048)
        k = 6 * f + 8 if f < FC - 1 else ITEM_UNITS - 2
        part = w_down[:, 512 * f:512 * f + 512, :].reshape(n, 2, 2, P, D).transpose(0, 1, 3, 2, 4)
        stream[:, k:k + 2] = part.reshape(n, 2, P, 2048)
    return stream


def build(nc, x, consts, ln_in, w_mix, b_forget, lam_qk, diff_g,
          ln_mix, ln_ffn, w_router, b_router, w_item, out):
    with ExitStack() as ctx:
        cursor = [18 * 1024]

        def at(name, shape, dt, offset):
            return nc.alloc_sbuf_tensor_at(name, shape, dt, offset=offset)

        def place(name, shape, dt=F32):
            offset = cursor[0]
            cursor[0] += (int(np.prod(shape[1:])) * 4 + 31) // 32 * 32
            return at(name, shape, dt, offset)

        raw_at = cursor[0]
        raw = place("raw", [P, RING, 2048])
        w_lo = at("w_lo", [P, RING, 2048], F32R, raw_at)
        w_hi = place("w_hi", [P, HRING, 2048], F32R)
        h = place("h", [P, TILES, D])
        act_hi = place("act_hi", [P, KT, SEQ], F32R)
        act_lo = place("act_lo", [P, KT, SEQ], F32R)
        cst = place("cst", [P, N_CONST])
        cat = place("cat", [P, TILES, D])
        small = place("small", [P, 2000])
        shared_at = cursor[0]
        gates = place("gates", [P, TILES, 3, D])
        v_sb = place("v_sb", [P, TILES, D])
        qkT_at = cursor[0]
        qkT = place("qkT", [P, 16, SEQ])
        p_at = cursor[0]
        prob_even = place("prob_even", [P, 2048])
        prob_odd = place("prob_odd", [P, 1024])
        sb_tmp = place("sb_tmp", [P, 1024])
        wT = place("wT", [P, 2, 4, P])
        sq = place("sq", [P, 512])
        q_stage = at("q_stage", [P, 2, TILES, 512], F32, p_at)
        end_mixer = cursor[0]
        mrg_hi = at("mrg_hi", [P, KT, SEQ], F32R, qkT_at)
        mrg_lo = at("mrg_lo", [P, KT, SEQ], F32R, qkT_at + KT * SEQ * 4)
        ln_gb = at("ln_gb", [P, 2, D], F32, p_at)
        cursor[0] = shared_at
        x_hi = place("x_hi", [P, KT, P], F32R)
        x_lo = place("x_lo", [P, KT, P], F32R)
        sig = place("sig", [P, 512])
        gsig = place("gsig", [P, 512])
        hid = place("hid", [P, 512])
        hid_hi = place("hid_hi", [P, 4, P], F32R)
        hid_lo = place("hid_lo", [P, 4, P], F32R)
        d_sb = place("d_sb", [P, D])
        scat = place("scat", [P, TILES, P])
        gath = place("gath", [P, TILES, P])
        rt = place("rt", [P, 512])
        assert cursor[0] <= qkT_at and end_mixer <= 229344

        zero_w = ctx.enter_context(nc.sbuf_tensor("zero_w", [P, P], F32R))

        def c(name):
            a, b = COLS[name]
            return cst[:, a:b]

        ident = c("ident")
        iota = c("iota")
        tri = c("tri").rearrange("p (k s) -> p k s", k=TILES)

        used = [0]

        def scratch(n):
            a = used[0]
            used[0] += n
            return small[:, a:a + n]

        lamq = scratch(DEPTH * 4 * HD).rearrange("p (l m d) -> p l m d", l=DEPTH, m=4)
        diffg = scratch(P)
        bf2 = scratch(DEPTH * NF).rearrange("p (l f) -> p l f", l=DEPTH)
        diffg2 = scratch(DEPTH * P).rearrange("p (l f) -> p l f", l=DEPTH)
        b_rt = scratch(N_EXP)
        bf = scratch(NF)
        lam_s = scratch(2)
        lam_e = scratch(2)
        lam = scratch(1)
        lq = scratch(4 * HD).rearrange("p (m d) -> p m d", m=4)
        lprod = scratch(2 * HD).rearrange("p (m d) -> p m d", m=2)
        neg_lam = scratch(1)
        lay = scratch(4)
        mv = scratch(TILES * 2).rearrange("p (t m) -> p t m", t=TILES)
        bst = scratch(TILES * 12).rearrange("p (t c m) -> p t c m", t=TILES, c=2)
        rv = scratch(4)
        rr = scratch(4)
        rn = scratch(4)
        f_x = scratch(8)
        f_l = scratch(8)
        lf = scratch(8).rearrange("p (t m) -> p t m", t=TILES)
        f_col = scratch(8).rearrange("p (t m) -> p t m", t=TILES)
        negmax = scratch(8)
        psum_s = scratch(8)
        rsum = scratch(8)
        f_row = scratch(SEQ)
        lg_row = scratch(SEQ)
        assert used[0] <= 2000

        rused = [0]

        def route(n):
            a = rused[0]
            rused[0] += n
            return rt[:, a:a + n]

        lg = route(16).rearrange("p (t e) -> p t e", t=TILES)
        lg2 = route(16).rearrange("p (t e) -> p t e", t=TILES)
        eq = route(16).rearrange("p (t e) -> p t e", t=TILES)
        oh1 = route(16).rearrange("p (t e) -> p t e", t=TILES)
        oh2 = route(16).rearrange("p (t e) -> p t e", t=TILES)
        sel = route(16).rearrange("p (t e) -> p t e", t=TILES)
        cwe = route(16).rearrange("p (t e) -> p t e", t=TILES)
        rkm = route(16).rearrange("p (t e) -> p t e", t=TILES)
        m1 = route(2).rearrange("p (t e) -> p t e", t=TILES)
        m2 = route(2).rearrange("p (t e) -> p t e", t=TILES)
        fi = route(2).rearrange("p (t e) -> p t e", t=TILES)
        dd = route(2).rearrange("p (t e) -> p t e", t=TILES)
        ee = route(2).rearrange("p (t e) -> p t e", t=TILES)
        w1 = route(2).rearrange("p (t e) -> p t e", t=TILES)
        w2 = route(2).rearrange("p (t e) -> p t e", t=TILES)
        ov = route(N_EXP)
        inc = route(N_EXP)
        exc = route(N_EXP)
        osel = route(N_EXP)
        prod = route(16).rearrange("p (t e) -> p t e", t=TILES)
        tab_rk = route(TILES * ITEM_COLS).rearrange("p (t i) -> p t i", t=TILES)
        tab_cw = route(TILES * ITEM_COLS).rearrange("p (t i) -> p t i", t=TILES)
        item_rk = route(TILES * ITEM_COLS).rearrange("p (t i) -> p t i", t=TILES)
        item_cw = route(TILES * (ITEM_COLS + 1)).rearrange("p (t i) -> p t i", t=TILES)
        ftab = route(ITEM_COLS + 1)
        wrb = route(N_EXP)
        assert rused[0] <= 512
        itab = ctx.enter_context(nc.sbuf_tensor("itab", [P, 16], I32))
        wr_hi = ctx.enter_context(nc.sbuf_tensor("wr_hi", [P, KT, N_EXP], F32R))
        wr_lo = ctx.enter_context(nc.sbuf_tensor("wr_lo", [P, KT, N_EXP], F32R))
        w_rt = ctx.enter_context(nc.sbuf_tensor("w_rt", [P, KT, N_EXP], F32))

        ps = ctx.enter_context(nc.psum_tensor("ps", [P, 8, 512], F32))

        def sem(name):
            return ctx.enter_context(nc.semaphore(name))

        s_raw = [sem(f"raw_loaded_{s}") for s in range(RING)]
        s_hi = sem("hi_split")
        s_lo = sem("lo_split")
        s_used = sem("unit_used")
        s_cst = sem("const_loaded")
        s_par = sem("params_loaded")
        s_x = sem("x_loaded")
        s_gb = sem("ln_params_loaded")
        s_lnd = sem("ln_params_used")
        s_h = sem("h_ready")
        s_tp = sem("transposed")
        s_tph = sem("transposed_hi")
        s_tpl = sem("transposed_lo")
        s_rv = sem("variance_ready")
        s_rr = sem("rsqrt_seeded")
        s_lam = sem("lambda_sums")
        s_lame = sem("lambda_exps")
        s_rope = sem("rope_done")
        s_qev = sem("qkv_copied")
        s_qt = sem("qk_transposed")
        s_qte = sem("qk_copied")
        s_fx = sem("forget_logit")
        s_fln = sem("forget_softplus")
        s_lf = sem("log_forget")
        s_F = sem("forget_sums")
        s_Fr = sem("forget_row_copied")
        s_Fc = sem("forget_col_copied")
        s_sc = sem("scores_done")
        s_scr = sem("scores_read")
        s_sbl = sem("sb_log_done")
        s_ei = sem("exp_input")
        s_ex = sem("exp_done")
        s_w = sem("weights_ready")
        s_wt = sem("weights_transposed")
        s_wte = sem("weights_copied")
        s_pv = sem("pv_done")
        s_pve = sem("pv_copied")
        s_rms = sem("rms_done")
        s_gl = sem("gate_logits_copied")
        s_sg = sem("gates_done")
        s_gm = sem("branches_gated")
        s_pch = sem("first_branches_added")
        s_mrg = sem("merged")
        s_wrh = sem("router_weights_hi")
        s_wrl = sem("router_weights_lo")
        s_lgr = sem("router_logit_rows")
        s_lgc = sem("router_logit_rows_copied")
        s_lg = sem("router_logits")
        s_rd = sem("router_gap")
        s_re = sem("router_exp")
        s_sel = sem("experts_selected")
        s_rk = sem("ranks_summed")
        s_tab = sem("items_listed")
        s_S = sem("gather_matrix")
        s_ga = sem("tokens_gathered")
        s_xh = sem("gathered_hi")
        s_xl = sem("gathered_lo")
        s_sig = sem("sigmoid_done")
        s_gs = sem("gate_silu")
        s_hd = sem("hidden_ready")
        s_tr = sem("hidden_transposed")
        s_th = sem("hidden_hi")
        s_tl = sem("hidden_lo")
        s_dA = sem("down_copied_left")
        s_dV = sem("down_copied_right")
        s_sT = sem("scatter_transposed")
        s_sTe = sem("scatter_copied")
        s_cb = sem("item_scattered")
        s_ac = sem("item_added")
        s_dch = sem("vector_chain")
        s_ach = sem("scalar_chain")
        s_zero = sem("zeros_ready")
        s_passed = sem("waits_passed")
        s_out = sem("output_stored")

        DVE_LAYER = 135
        ACT_LAYER = 10

        def hold(eng, semaphore, value):
            eng.wait_ge(semaphore, value)
            eng.sem_inc(s_passed, 1)

        def groups_of(kind, t):
            return (8 if kind == "diff" else 4), P * (t + 1)

        def place_of(g, j):
            return j % 2 * (groups_of(*GROUPS[g])[0] // 2) + j // 2

        def scores_of(g):
            m, keys = groups_of(*GROUPS[g])
            half = m * keys // 2
            if half >= 512:
                return ps[:, BANK[g]:BANK[g] + half // 256, :].rearrange("p (a b) n -> p a (b n)", a=2)
            return ps[:, BANK[g]:BANK[g] + 2, 0:half]

        def turned_bank(g, r):
            return 6 + (r if GROUPS[g][1] else g % 2)

        def heads_bank(g):
            return 6 if GROUPS[g][1] else 6 + g % 2

        def prob(g):
            return (prob_odd if g % 2 else prob_even)

        block = ctx.enter_context(nc.Block())

        @block.sync
        def _(sp):
            sp.dma_start(h[:], x[0].rearrange("(t p) d -> p t d", p=P)).then_inc(s_x, 16)
            sp.dma_start(cst[:], consts[:, :]).then_inc(s_cst, 16)

            def load(base, k, src):
                hold(sp, s_used, base + (k + 1))
                sp.dma_start(raw[:, k % RING, 0:src.shape[-1]], src).then_inc(s_raw[k % RING], 16)

            def item_units(base, e, ks):
                for k in ks:
                    load(base, k, w_item[bass.ds(e, 1), k].rearrange("a p n -> p (a n)"))

            with sp.Fori(0, DEPTH) as l:
                base = l * LAYER_UNITS
                for k in range(MIX_UNITS):
                    load(base, k, w_mix[bass.ds(l, 1), k, :, 0:mix_words(k)].rearrange("a p n -> p (a n)"))
                first = base + MIX_UNITS
                item_units(first, l, range(6))
                hold(sp, s_tab, l + 1)
                n = sp.value_load(itab[0:1, 0:1], min_val=2, max_val=ITEMS)
                with sp.Fori(0, n - 1) as i:
                    ib = l * LAYER_UNITS + i * ITEM_UNITS + MIX_UNITS
                    e = sp.value_load(itab[0:1, bass.ds(i + 1, 1)], min_val=0, max_val=N_EXP)
                    item_units(ib, e, range(6, ITEM_UNITS))
                    e2 = sp.value_load(itab[0:1, bass.ds(i + 2, 1)], min_val=0, max_val=N_EXP)
                    item_units(ib + ITEM_UNITS, e2, range(6))
                e = sp.value_load(itab[0:1, bass.ds(n, 1)], min_val=0, max_val=N_EXP)
                item_units(l * LAYER_UNITS + (n - 1) * ITEM_UNITS + MIX_UNITS, e, range(6, ITEM_UNITS))
            n = sp.value_load(itab[0:1, 0:1], min_val=2, max_val=ITEMS)
            for k in range(HRING):
                load(LAYER_UNITS + MIX_UNITS + n * ITEM_UNITS, k, w_mix[0, k])
            sp.wait_ge(s_h, TILES * (1 + 2 * DEPTH))
            sp.dma_start(out[0].rearrange("(t p) d -> p t d", p=P), h[:]).then_inc(s_out, 16)
            sp.wait_ge(s_out, 16)

        @block.gpsimd
        def _(pool):
            pool.dma_start(ln_gb[:], ln_in.rearrange("(o m) d -> o m d", o=1).to_broadcast([P, 2, D])).then_inc(s_gb, 16)
            nc.gpsimd.memset(zero_w[:].bitcast(F32), 0.0).then_inc(s_zero, 1)
            pool.dma_start(lamq, lam_qk.rearrange("(o l) m d -> o l m d", o=1).to_broadcast([P, DEPTH, 4, HD])).then_inc(s_par, 16)
            pool.dma_start(bf2, b_forget.rearrange("(o l) f -> o l f", o=1).to_broadcast([P, DEPTH, NF])).then_inc(s_par, 16)
            pool.dma_start(diffg2, diff_g.rearrange("(o l) f -> o l f", o=1).to_broadcast([P, DEPTH, P])).then_inc(s_par, 16)
            pool.dma_start(b_rt, b_router.to_broadcast([P, N_EXP])).then_inc(s_par, 16)
            pool.dma_start(w_rt[:], w_router[0].rearrange("(k p) e -> p k e", p=P)).then_inc(s_par, 16)
            with pool.Fori(0, DEPTH) as l:
                hold(pool, s_tpl, l * 16 + 8)
                pool.dma_start(ln_gb[:], ln_mix[bass.ds(l, 1)].to_broadcast([P, 2, D])).then_inc(s_gb, 16)
                for cc in range(2):
                    def part(t, b):
                        return gates[:, t, b, 512 * cc:512 * cc + 512]

                    hold(pool, s_gm, l * 6 + (3 * cc + 2))
                    for t in range(TILES):
                        nc.gpsimd.tensor_tensor(cat[:, t, 512 * cc:512 * cc + 512], part(t, 0), part(t, 1), ALU.add).then_inc(s_pch, 1)
                    hold(pool, s_gm, l * 6 + (3 * cc + 3))
                    hold(pool, s_pch, l * 4 + (2 * cc + 2))
                    for t in range(TILES):
                        m = cat[:, t, 512 * cc:512 * cc + 512]
                        nc.gpsimd.tensor_tensor(m, m, part(t, 2), ALU.add).then_inc(s_mrg, 1)
                hold(pool, s_lnd, l * 2 + 2)
                pool.dma_start(ln_gb[:], ln_ffn[bass.ds(l, 1)].to_broadcast([P, 2, D])).then_inc(s_gb, 16)

        @block.scalar
        def _(act):
            link_count = [0, 0]

            def link(ins):
                link_count[1] += 1
                ins.then_inc(s_ach, 1)
                act.wait_ge(s_ach, link_count[0] + link_count[1])

            def split(nb, qb, k, n=2048):
                act.wait_ge(s_raw[k % RING], (qb + (k // RING + 1)) * 16)
                act.wait_ge(s_used, nb + (k + RING - HRING + 1))
                nc.scalar.activation(w_hi[:, k % HRING, 0:n], raw[:, k % RING, 0:n], ACT.Copy).then_inc(s_hi, 1)

            def rsqrt_seed(index, n):
                act.wait_ge(s_rv, index + 1)
                link(nc.scalar.activation(rr[:, 0:n], rv[:, 0:n], ACT.Ln))
                nc.scalar.activation(rr[:, 0:n], rr[:, 0:n], ACT.Exp, scale=-0.5).then_inc(s_rr, 1)

            def transposed_hi(job, hi, steps=range(4), layout=JOB):
                for step in steps:
                    t, half, bank = layout[step]
                    act.wait_ge(s_tp, job * 4 + (step + 1))
                    nc.scalar.activation(hi[:, 4 * half:4 * half + 4, t * P:t * P + P],
                                         ps[:, bank, :].rearrange("p (k n) -> p k n", k=4),
                                         ACT.Copy).then_inc(s_tph, 1)

            nc.scalar.sem_inc(s_dA, 1)
            nc.scalar.sem_inc(s_sTe, 1)
            rsqrt_seed(0, TILES)
            split(0, 0, 0)
            transposed_hi(0, act_hi)
            split(0, 0, 1)
            split(0, 0, 2)

            with act.Fori(0, DEPTH) as l:
                nb, qb = l * LAYER_UNITS, l * (LAYER_UNITS // RING)
                link_count[0], link_count[1] = l * ACT_LAYER + 1, 0

                def qk_copy(j):
                    act.wait_ge(s_qt, l * 5 + (j + 1))
                    parts = {0: [(0, 4, 0.125)], 1: [(4, 4, 1.0)], 2: [(8, 2, 0.125), (10, 2, 1.0)],
                             3: [(12, 2, 0.125)], 4: [(14, 2, 1.0)]}[j]
                    for t in range(TILES):
                        for b0, nblk, scale in parts:
                            o = (b0 - parts[0][0]) * P
                            ins = nc.scalar.activation(
                                qkT[:, b0:b0 + nblk, t * P:t * P + P],
                                ps[:, 4 + t, o:o + nblk * P].rearrange("p (b n) -> p b n", b=nblk),
                                ACT.Copy, scale=scale)
                    ins.then_inc(s_qte, 1)

                for cc in range(6):
                    split(nb, qb, 2 * cc + 3, mix_words(2 * cc + 3))
                    split(nb, qb, 2 * cc + 4, mix_words(2 * cc + 4))
                    if cc >= 2:
                        act.wait_ge(s_used, nb + (2 * cc + 1 + RING + 1))
                        if cc >= 3:
                            act.wait_ge(s_qt, l * 5 + (cc - 2))
                        b = 2 * (cc % 2)
                        slot = {3: 0, 4: 1, 5: 0}.get(cc)
                        for t in range(TILES):
                            src = ps[:, b + t, :]
                            if cc == 2:
                                ins = nc.scalar.activation(v_sb[:, t, 0:512], src, ACT.Copy)
                            elif cc == 3:
                                ins = nc.scalar.activation(q_stage[:, slot, t, :], src, ACT.Copy)
                            elif cc == 4:
                                nc.scalar.activation(v_sb[:, t, 512:768], src[:, 0:256], ACT.Copy)
                                ins = nc.scalar.activation(q_stage[:, slot, t, 0:256], src[:, 256:512], ACT.Copy)
                            else:
                                nc.scalar.activation(v_sb[:, t, 768:1024], src[:, 256:512], ACT.Copy)
                                ins = nc.scalar.activation(q_stage[:, slot, t, 0:256], src[:, 0:256], ACT.Copy)
                        ins.then_inc(s_qev, 1)
                    if cc in (1, 2, 4, 5):
                        qk_copy({1: 0, 2: 1, 4: 2, 5: 3}[cc])
                split(nb, qb, 15)
                split(nb, qb, 16)
                qk_copy(4)
                act.wait_ge(s_par, 16 * PARAM_LOADS)
                nc.scalar.activation(wr_hi[:], w_rt[:], ACT.Copy).then_inc(s_wrh, 1)
                act.wait_ge(s_lam, l + 1)
                nc.scalar.activation(lam_e, lam_s, ACT.Exp).then_inc(s_lame, 1)
                act.wait_ge(s_fx, l + 1)
                link(nc.scalar.activation(f_l, f_x, ACT.Abs))
                link(nc.scalar.activation(f_l, f_l, ACT.Exp, scale=-1.0))
                nc.scalar.activation(f_l, f_l, ACT.Ln, bias=1.0).then_inc(s_fln, 1)

                def gates_copy(g):
                    act.wait_ge(s_used, nb + (U_GATE + 2 * g + 1 + RING + 1))
                    for t in range(TILES):
                        ins = nc.scalar.activation(gates[:, t, g // 2, 512 * (g % 2):512 * (g % 2) + 512],
                                                   ps[:, t, :], ACT.Copy)
                    ins.then_inc(s_gl, 1)

                def exps_first(g):
                    kind, t = GROUPS[g]
                    m, keys = groups_of(kind, t)
                    if kind == "sb":
                        act.wait_ge(s_sc, l * 6 + (g + 1))
                        if g >= 2:
                            act.wait_ge(s_wt, l * ROUNDS + ROUNDS_BEFORE[g - 1])
                        buf = prob(g)[:, 0:m * keys]
                        link(nc.scalar.activation(buf.rearrange("p (a n) -> p a n", a=2), scores_of(g), ACT.Abs))
                        link(nc.scalar.activation(buf, buf, ACT.Exp, scale=-1.0))
                        nc.scalar.activation(buf, buf, ACT.Ln, bias=1.0).then_inc(s_sbl, 1)

                def exps(g):
                    kind, t = GROUPS[g]
                    m, keys = groups_of(kind, t)
                    act.wait_ge(s_ei, l * 6 + (g + 1))
                    buf = prob(g)
                    if kind == "sb":
                        nc.scalar.activation(buf[:, 0:m * keys], sb_tmp[:, 0:m * keys], ACT.Exp).then_inc(s_ex, 1)
                        return
                    for j in range(m):
                        ins = nc.scalar.activation(buf[:, j * keys:(j + 1) * keys], buf[:, j * keys:(j + 1) * keys],
                                                   ACT.Exp, bias=negmax[:, j:j + 1], accum_out=psum_s[:, j:j + 1])
                    ins.then_inc(s_ex, 1)

                def turned_copy(g):
                    for r in range(GROUPS[g][1] + 1):
                        bank = turned_bank(g, r)
                        act.wait_ge(s_wt, l * ROUNDS + (ROUNDS_BEFORE[g] + r + 1))
                        nc.scalar.activation(wT[:, bank - 6, :, :], ps[:, bank, :].rearrange("p (h n) -> p h n", h=4),
                                             ACT.Copy).then_inc(s_wte, 1)

                def heads_copy(g):
                    kind, t = GROUPS[g]
                    width = 512 if kind == "diff" else 256
                    act.wait_ge(s_pv, l * 6 + (g + 1))
                    nc.scalar.activation(cat[:, t, CAT_OFF[kind]:CAT_OFF[kind] + width], ps[:, heads_bank(g), 0:width],
                                         ACT.Copy).then_inc(s_pve, 1)

                split(nb, qb, U_GATE + 3)
                gates_copy(0)
                act.wait_ge(s_F, l + 1)
                nc.scalar.activation(f_row[0:NF, :], ps[0:NF, 6, 0:SEQ], ACT.Copy).then_inc(s_Fr, 1)
                exps(0)
                split(nb, qb, U_GATE + 4)
                for g in range(1, 6):
                    exps_first(g)
                    split(nb, qb, U_GATE + 2 * g + 3, mix_words(U_GATE + 2 * g + 3))
                    if g >= 2:
                        heads_copy(g - 2)
                    exps(g)
                    gates_copy(g)
                    split(nb, qb, U_GATE + 2 * g + 4, mix_words(U_GATE + 2 * g + 4))
                    turned_copy(g - 1)
                    if g in (2, 5):
                        rsqrt_seed(l * 4 + (1 if g == 2 else 2), 4)
                transposed_hi(l * 4 + 1, act_hi, (0, 1), HEADS_JOB)
                turned_copy(5)
                heads_copy(4)
                transposed_hi(l * 4 + 1, act_hi, (2,), HEADS_JOB)
                heads_copy(5)
                transposed_hi(l * 4 + 1, act_hi, (3,), HEADS_JOB)
                for cc in range(2):
                    for t in range(TILES):
                        part = gates[:, t, :, 512 * cc:512 * cc + 512]
                        nc.scalar.activation(part, part, ACT.Sigmoid).then_inc(s_sg, 1)
                for k in range(U_UP, U_OUT + 4):
                    split(nb, qb, k + 3, mix_words(k + 3) if k + 3 < MIX_UNITS else 2048)
                    if k == U_UP + 4:
                        transposed_hi(l * 4 + 2, mrg_hi, (0, 1), MERGED_JOB)
                    if k == U_OUT:
                        transposed_hi(l * 4 + 2, mrg_hi, (2, 3), MERGED_JOB)
                rsqrt_seed(l * 4 + 3, TILES)
                transposed_hi(l * 4 + 3, act_hi)

                act.wait_ge(s_lgr, l + 1)
                nc.scalar.activation(lg_row[0:N_EXP, :], ps[0:N_EXP, 6, 0:SEQ], ACT.Copy).then_inc(s_lgc, 1)
                act.wait_ge(s_rd, l + 1)
                nc.scalar.activation(ee, dd, ACT.Exp).then_inc(s_re, 1)

                def gathered_hi(index):
                    for b in range(2):
                        act.wait_ge(s_ga, index * 2 + (b + 1))
                        nc.scalar.activation(x_hi[:, 4 * b:4 * b + 4, :],
                                             ps[:, 1 + 2 * b, :].rearrange("p (k n) -> p k n", k=4),
                                             ACT.Copy).then_inc(s_xh, 1)

                gathered_hi(l * (DENSE_ITEMS + 1))
                hold(act, s_tab, l + 1)
                n_items = act.value_load(itab[0:1, 0:1], min_val=2, max_val=ITEMS)
                with act.Fori(0, n_items) as i:
                    item = l * DENSE_ITEMS + i
                    inb = l * LAYER_UNITS + i * ITEM_UNITS + MIX_UNITS
                    iqb = l * (LAYER_UNITS // RING) + i * (ITEM_UNITS // RING) + MIX_UNITS // RING
                    it7 = item * FC

                    def sigmoid(ub, u_done, f_par):
                        act.wait_ge(s_used, ub + (u_done + RING + 1))
                        nc.scalar.activation(sig[:], ps[:, f_par, :], ACT.Sigmoid).then_inc(s_sig, 1)

                    def hidden_hi(count):
                        act.wait_ge(s_tr, count)
                        nc.scalar.activation(hid_hi[:], ps[:, 6, :].rearrange("p (k n) -> p k n", k=4),
                                             ACT.Copy).then_inc(s_th, 1)

                    split(inb, iqb, 3)
                    split(inb, iqb, 4)
                    sigmoid(inb, 1, 0)
                    split(inb, iqb, 5)
                    split(inb, iqb, 6)
                    act.wait_ge(s_sT, item + 1)
                    nc.scalar.activation(scat[:], ps[:, 0, 0:TILES * P].rearrange("p (t n) -> p t n", t=TILES),
                                         ACT.Copy).then_inc(s_sTe, 1)
                    with act.Fori(0, FC // 2) as j:
                        jnb, jqb = inb + j * 12, iqb + j * 2
                        for u in range(2):
                            k0 = 4 + 6 * u
                            done = it7 + j * 2 + u
                            split(jnb, jqb, k0 + 3)
                            split(jnb, jqb, k0 + 4)
                            hidden_hi(done + 1)
                            act.wait_ge(s_gs, done + 1)
                            sigmoid(jnb, k0 + 1, (u + 1) % 2)
                            split(jnb, jqb, k0 + 5)
                            split(jnb, jqb, k0 + 6)
                            split(jnb, jqb, k0 + 7)
                            split(jnb, jqb, k0 + 8)
                    hidden_hi(it7 + FC)
                    gathered_hi(item + l + 1)
                    split(inb, iqb, ITEM_UNITS + 1)
                    act.wait_ge(s_used, inb + (ITEM_UNITS - 1 + RING + 1))
                    nc.scalar.activation(d_sb[:, 0:512], ps[:, 4, :], ACT.Copy).then_inc(s_dA, 1)
                    split(inb, iqb, ITEM_UNITS + 2)
                rsqrt_seed(l * 4 + 4, TILES)
                transposed_hi(l * 4 + 4, act_hi)
                assert link_count[1] == ACT_LAYER

        @block.vector
        def _(dve):
            link_count = [0, 0]

            def link(ins):
                link_count[1] += 1
                ins.then_inc(s_dch, 1)
                dve.wait_ge(s_dch, link_count[0] + link_count[1])

            def split(nb, k, n=2048):
                dve.wait_ge(s_hi, nb + (k + 1))
                nc.vector.tensor_tensor(w_lo[:, k % RING, 0:n], raw[:, k % RING, 0:n],
                                        w_hi[:, k % HRING, 0:n].bitcast(F32), ALU.subtract).then_inc(s_lo, 1)

            def refine(index, n, out_ap):
                dve.wait_ge(s_rr, index + 1)
                link(nc.vector.tensor_tensor(rn[:, 0:n], rr[:, 0:n], rr[:, 0:n], ALU.mult))
                link(nc.vector.tensor_tensor(rn[:, 0:n], rn[:, 0:n], rv[:, 0:n], ALU.mult))
                link(nc.vector.tensor_scalar(rn[:, 0:n], rn[:, 0:n], -0.5, 1.5, ALU.mult, ALU.add))
                link(nc.vector.tensor_tensor(out_ap, rn[:, 0:n], rr[:, 0:n], ALU.mult))

            def statistics(src, t, b):
                link(nc.vector.bn_stats(bst[:, t, b, :], src[:, t, 512 * b:512 * b + 512]))

            def normalise(index, ln_index, src, meanwhile=None):
                for t in range(TILES):
                    dve.sem_inc(s_passed, 1)
                    link(nc.vector.bn_aggr(mv[:, t, :], bst[:, t].rearrange("p c m -> p (c m)")))
                nc.vector.tensor_scalar(rv[:, 0:TILES], mv[:, :, 1], 1e-5, None, ALU.add).then_inc(s_rv, 1)
                if meanwhile:
                    meanwhile()
                refine(index, TILES, rn[:, 0:TILES])
                dve.wait_ge(s_gb, (ln_index + 1) * 16)
                for t in range(TILES):
                    link(nc.vector.tensor_scalar(h[:, t, :], src[:, t, :], mv[:, t, 0:1], rn[:, t:t + 1],
                                                 ALU.subtract, ALU.mult))
                    link(nc.vector.tensor_tensor(h[:, t, :], h[:, t, :], ln_gb[:, 0, :], ALU.mult))
                    ins = nc.vector.tensor_tensor(h[:, t, :], h[:, t, :], ln_gb[:, 1, :], ALU.add)
                    ins.then_inc(s_h, 1)
                dve.wait_ge(s_h, (ln_index + 1) * TILES)
                dve.sem_inc(s_lnd, 1)

            def transposed_lo(job, hi, lo, steps=range(4), layout=JOB):
                for step in steps:
                    t, half, bank = layout[step]
                    dve.wait_ge(s_tph, job * 4 + (step + 1))
                    part = (slice(None), slice(4 * half, 4 * half + 4), slice(t * P, t * P + P))
                    nc.vector.tensor_tensor(lo[part], ps[:, bank, :].rearrange("p (k n) -> p k n", k=4),
                                            hi[part].bitcast(F32), ALU.subtract).then_inc(s_tpl, 1)

            dve.sem_inc(s_dV, 1)
            dve.wait_ge(s_x, 16)
            for t in range(TILES):
                for b in range(2):
                    statistics(h, t, b)
            normalise(0, 0, h)
            split(0, 0)
            transposed_lo(0, act_hi, act_lo)
            split(0, 1)
            split(0, 2)
            dve.wait_ge(s_cst, 16)
            before_loop = link_count[1]

            with dve.Fori(0, DEPTH) as l:
                nb = l * LAYER_UNITS
                link_count[0], link_count[1] = l * DVE_LAYER + before_loop, 0

                def rope(cc):
                    dve.wait_ge(s_used, nb + (2 * cc + 1 + RING + 1))
                    for t in range(TILES):
                        src = ps[:, 2 * cc + t, :].rearrange("p (m h d) -> p m h d", m=8, h=2)
                        dst = q_stage[:, cc, t, :].rearrange("p (m h d) -> p m h d", m=8, h=2)
                        swp = sb_tmp[:, 512 * (t % 2):512 * (t % 2) + 512].rearrange("p (m h d) -> p m h d", m=8, h=2)

                        def table(name, hh):
                            a = COLS[name][0] + HD * t + HD // 2 * hh
                            return cst[:, a:a + HD // 2].unsqueeze(1).to_broadcast([P, 8, HD // 2])

                        for hh in range(2):
                            nc.vector.tensor_tensor(dst[:, :, hh, :], src[:, :, hh, :], table("cos", hh), ALU.mult)
                            ins = nc.vector.tensor_tensor(swp[:, :, hh, :], src[:, :, 1 - hh, :], table("sin", hh), ALU.mult)
                        link(ins)
                        nc.vector.tensor_tensor(q_stage[:, cc, t, :], q_stage[:, cc, t, :],
                                                sb_tmp[:, 512 * (t % 2):512 * (t % 2) + 512], ALU.add).then_inc(s_rope, 1)

                for cc in range(6):
                    split(nb, 2 * cc + 3, mix_words(2 * cc + 3))
                    split(nb, 2 * cc + 4, mix_words(2 * cc + 4))
                    if cc < 2:
                        rope(cc)
                split(nb, 15)
                split(nb, 16)
                dve.wait_ge(s_par, 16 * PARAM_LOADS)
                a = COLS["layer"][0]
                nc.vector.tensor_copy(bf, bf2[:, bass.ds(l, 1), :].rearrange("p a m -> p (a m)"))
                nc.vector.tensor_copy(lay, cst[:, a:a + 4 * DEPTH].rearrange("p (l m) -> p l m", l=DEPTH)[:, bass.ds(l, 1), :]
                                      .rearrange("p a m -> p (a m)"))
                link(nc.vector.tensor_copy(lq, lamq[:, bass.ds(l, 1), :, :].rearrange("p a m d -> p (a m) d")))
                pairs = lq.rearrange("p (m two) d -> p m two d", two=2)
                link(nc.vector.tensor_tensor(lprod, pairs[:, :, 0, :], pairs[:, :, 1, :], ALU.mult))
                nc.vector.tensor_reduce(lam_s, lprod, AX, ALU.add).then_inc(s_lam, 1)
                nc.vector.tensor_scalar(diffg, diffg2[:, bass.ds(l, 1), :].rearrange("p a m -> p (a m)"),
                                        lay[:, 1:2], None, ALU.mult)
                dve.wait_ge(s_used, nb + (U_F + 1 + RING + 1))
                for t in range(TILES):
                    ins = nc.vector.tensor_tensor(f_x[:, NF * t:NF * t + NF], ps[:, 6 + t, 0:NF], bf, ALU.add)
                ins.then_inc(s_fx, 1)
                dve.wait_ge(s_fln, l + 1)
                nc.vector.scalar_tensor_tensor(lf.rearrange("p t f -> p (t f)"), f_x, 0.0, f_l, ALU.min, ALU.subtract).then_inc(s_lf, 1)
                dve.wait_ge(s_wrh, l + 1)
                nc.vector.tensor_tensor(wr_lo[:], w_rt[:], wr_hi[:].bitcast(F32), ALU.subtract).then_inc(s_wrl, 1)
                dve.wait_ge(s_lame, l + 1)
                link(nc.vector.tensor_tensor(lam, lam_e[:, 0:1], lam_e[:, 1:2], ALU.subtract))
                link(nc.vector.tensor_scalar(neg_lam, lam, lay[:, 0:1], -1.0, ALU.add, ALU.mult))

                def group_first(g):
                    kind, t = GROUPS[g]
                    m, keys = groups_of(kind, t)
                    buf = prob(g)[:, 0:m * keys]
                    b3 = buf.rearrange("p (m k) -> p m k", m=m)
                    mask = {"diff": c(f"mdiff{t}"), "fox": c(f"mfox{t}"), "sb": c(f"msb{t}")}[kind]
                    mask3 = mask.unsqueeze(1).to_broadcast([P, m, keys])
                    z = scores_of(g)

                    def halves(a):
                        return a.rearrange("p (a n) -> p a n", a=2)

                    def score(j):
                        pos = place_of(g, j)
                        o = pos % (m // 2) * keys
                        return z[:, pos // (m // 2), o:o + keys]

                    dve.wait_ge(s_sc, l * 6 + (g + 1))
                    if kind == "sb":
                        u = sb_tmp[:, 0:m * keys]
                        u3 = u.rearrange("p (m k) -> p m k", m=m)
                        dve.wait_ge(s_sbl, l * 2 + (1 if g == 1 else 2))
                        link(nc.vector.scalar_tensor_tensor(halves(u), z, 0.0, halves(buf), ALU.max, ALU.add))
                        link(nc.vector.scalar_tensor_tensor(u3, mask3, 0.0, u3, ALU.is_ge, ALU.mult))
                        for j in range(m):
                            ins = nc.vector.tensor_tensor_scan(b3[:, j, ::-1], u3[:, j, ::-1], u3[:, j, ::-1],
                                                               0.0, ALU.add, ALU.max)
                        link(ins)
                        ins = nc.vector.tensor_tensor(halves(u), z, halves(buf), ALU.subtract)
                        link(ins)
                        dve.sem_inc(s_scr, 1)
                        nc.vector.tensor_tensor(u3, u3, mask3, ALU.add).then_inc(s_ei, 1)
                        return
                    if g >= 2:
                        dve.wait_ge(s_wt, l * ROUNDS + ROUNDS_BEFORE[g - 1])
                    if kind == "diff":
                        ins = nc.vector.tensor_tensor(b3, z.rearrange("p a n -> p (a n)").rearrange("p (m k) -> p m k", m=m), mask3, ALU.add)
                    else:
                        if g == 2:
                            dve.wait_ge(s_Fc, l + 1)
                        for j in range(m):
                            ins = nc.vector.scalar_tensor_tensor(b3[:, place_of(g, j), :], score(j), f_col[:, t, j:j + 1],
                                                                 mask, ALU.add, ALU.add)
                    link(ins)
                    dve.sem_inc(s_scr, 1)
                    link(nc.vector.tensor_reduce(negmax[:, 0:m], b3, AX, ALU.max, negate=True))
                    dve.sem_inc(s_ei, 1)

                def group_last(g):
                    kind, t = GROUPS[g]
                    m, keys = groups_of(kind, t)
                    if kind == "sb":
                        return
                    b3 = prob(g)[:, 0:m * keys].rearrange("p (m k) -> p m k", m=m)
                    dve.wait_ge(s_ex, l * 6 + (g + 1))
                    link(nc.vector.reciprocal(rsum[:, 0:m], psum_s[:, 0:m]))
                    if kind == "diff":
                        link(nc.vector.tensor_scalar(rsum[:, 4:8], rsum[:, 4:8], neg_lam, None, ALU.mult))
                    ins = nc.vector.tensor_tensor(b3, b3, rsum[:, 0:m].unsqueeze(2).to_broadcast([P, m, keys]), ALU.mult)
                    if kind == "diff":
                        link(ins)
                        ins = nc.vector.tensor_tensor(b3[:, 0:4, :], b3[:, 0:4, :], b3[:, 4:8, :], ALU.add)
                    ins.then_inc(s_w, 1)

                def rms(g):
                    t = GROUPS[g][1]
                    index = l * 4 + (1 if g == 0 else 2)
                    o = cat[:, t, 0:512]
                    o3 = o.rearrange("p (h v) -> p h v", h=4)
                    dve.wait_ge(s_pve, l * 6 + (g + 1))
                    link(nc.vector.tensor_tensor(sq[:], o, o, ALU.mult))
                    link(nc.vector.tensor_reduce(rv[:, 0:4], sq[:].rearrange("p (h v) -> p h v", h=4), AX, ALU.add))
                    nc.vector.tensor_scalar(rv[:, 0:4], rv[:, 0:4], 1.0 / P, 1e-6, ALU.mult, ALU.add).then_inc(s_rv, 1)
                    refine(index, 4, rn[:, 0:4])
                    link(nc.vector.tensor_tensor(o3, o3, rn[:, 0:4].unsqueeze(2).to_broadcast([P, 4, P]), ALU.mult))
                    nc.vector.tensor_tensor(o3, o3, diffg.unsqueeze(1).to_broadcast([P, 4, P]), ALU.mult).then_inc(s_rms, 1)

                split(nb, U_GATE + 3)
                group_first(0)
                dve.wait_ge(s_F, l + 1)
                nc.vector.tensor_copy(f_col, ps[:, 7, 0:TILES * NF].rearrange("p (t f) -> p t f", t=TILES)).then_inc(s_Fc, 1)
                group_last(0)
                split(nb, U_GATE + 4)
                for g in range(1, 6):
                    group_first(g)
                    split(nb, U_GATE + 2 * g + 3, mix_words(U_GATE + 2 * g + 3))
                    group_last(g)
                    split(nb, U_GATE + 2 * g + 4, mix_words(U_GATE + 2 * g + 4))
                    if g in (2, 5):
                        rms(g - 2)
                transposed_lo(l * 4 + 1, act_hi, act_lo, range(4), HEADS_JOB)
                for cc in range(2):
                    for b in range(3):
                        k = U_UP + 3 * cc + b
                        split(nb, k + 3, mix_words(k + 3))
                        dve.wait_ge(s_used, nb + (k + RING + 1))
                        for t in range(TILES):
                            dve.wait_ge(s_sg, l * 4 + (2 * cc + t + 1))
                            gate = gates[:, t, b, 512 * cc:512 * cc + 512]
                            ins = nc.vector.tensor_tensor(gate, gate, ps[:, 2 * b + t, :], ALU.mult)
                        ins.then_inc(s_gm, 1)
                        if k == U_UP + 4:
                            transposed_lo(l * 4 + 2, mrg_hi, mrg_lo, (0, 1), MERGED_JOB)
                split(nb, U_OUT + 3)
                transposed_lo(l * 4 + 2, mrg_hi, mrg_lo, (2, 3), MERGED_JOB)
                split(nb, U_OUT + 4)
                split(nb, U_OUT + 5)
                for half in range(2):
                    dve.wait_ge(s_used, nb + (U_OUT + 2 + half + RING + 1))
                    for t in range(TILES):
                        part_h = h[:, t, 512 * half:512 * half + 512]
                        ins = nc.vector.scalar_tensor_tensor(part_h, part_h, ALPHA, ps[:, 2 * half + t, :], ALU.mult, ALU.add)
                    link(ins)
                    for t in range(TILES):
                        statistics(h, t, half)
                normalise(l * 4 + 3, l * 2 + 1, h, lambda: split(nb, U_OUT + 6))
                transposed_lo(l * 4 + 3, act_hi, act_lo)

                nc.vector.memset(d_sb[:], 0.0)
                nc.vector.memset(scat[:], 0.0)
                nc.vector.tensor_scalar(cat[:], h[:], ALPHA, None, ALU.mult)
                nc.vector.memset(tab_rk, -1.0)
                nc.vector.memset(tab_cw, 0.0)
                link(nc.vector.memset(item_cw, 0.0))
                e16 = [P, TILES, N_EXP]

                def wide(a):
                    return a.to_broadcast(e16)

                def cols(name):
                    return c(name).unsqueeze(1).to_broadcast(e16)

                dve.wait_ge(s_lg, l + 1)
                link(nc.vector.tensor_tensor(lg, ps[:, 7, 0:TILES * N_EXP].rearrange("p (t e) -> p t e", t=TILES),
                                             b_rt.unsqueeze(1).to_broadcast(e16), ALU.add))

                def first_largest(logits, largest, onehot):
                    link(nc.vector.tensor_reduce(largest.rearrange("p t e -> p (t e)"), logits, AX, ALU.max))
                    link(nc.vector.tensor_tensor(eq, logits, wide(largest), ALU.is_equal))
                    link(nc.vector.tensor_tensor(eq, eq, cols("first"), ALU.mult))
                    link(nc.vector.tensor_reduce(fi.rearrange("p t e -> p (t e)"), eq, AX, ALU.min))
                    link(nc.vector.tensor_tensor(onehot, cols("first"), wide(fi), ALU.is_equal))

                first_largest(lg, m1, oh1)
                link(nc.vector.scalar_tensor_tensor(lg2, oh1, -3e38, lg, ALU.mult, ALU.add))
                first_largest(lg2, m2, oh2)
                nc.vector.tensor_tensor(sel, oh1, oh2, ALU.add).then_inc(s_sel, 1)
                nc.vector.tensor_tensor(dd, m2, m1, ALU.subtract).then_inc(s_rd, 1)
                dve.wait_ge(s_re, l + 1)
                link(nc.vector.tensor_scalar(w1, ee, 1.0, None, ALU.add))
                link(nc.vector.reciprocal(w1, w1))
                link(nc.vector.tensor_tensor(w2, w1, ee, ALU.mult))
                link(nc.vector.tensor_tensor(cwe, oh1, wide(w1), ALU.mult))
                link(nc.vector.tensor_tensor(eq, oh2, wide(w2), ALU.mult))
                link(nc.vector.tensor_tensor(cwe, cwe, eq, ALU.add))
                dve.wait_ge(s_rk, l + 1)
                link(nc.vector.tensor_tensor(rkm, ps[:, 6, 0:TILES * N_EXP].rearrange("p (t e) -> p t e", t=TILES), sel, ALU.mult))
                link(nc.vector.tensor_scalar(rkm, rkm, -1.0, None, ALU.add))
                drk = c("drk").rearrange("p (t i) -> p t i", t=TILES)
                link(nc.vector.tensor_scalar(item_rk[:, :, 0:1], rkm[:, :, 0:1], lay[:, 2:3], None, ALU.mult))
                link(nc.vector.scalar_tensor_tensor(item_rk[:, :, 0:1], drk[:, :, 0:1], lay[:, 3:4], item_rk[:, :, 0:1], ALU.mult, ALU.add))

                def gather_matrix(i):
                    for t in range(TILES):
                        ins = nc.vector.tensor_scalar(gath[:, t, :], iota, item_rk[:, t, bass.ds(i, 1)], None, ALU.is_equal)
                    ins.then_inc(s_S, 1)

                gather_matrix(0)
                link(nc.vector.tensor_scalar(ov, ps[:, 7, 0:N_EXP], float(P), None, ALU.is_gt))
                link(nc.vector.tensor_tensor_scan(inc, ov, ov, 0.0, ALU.add, ALU.max))
                link(nc.vector.tensor_tensor(exc, inc, ov, ALU.subtract))
                link(nc.vector.tensor_copy(tab_rk[:, :, 0:N_EXP], rkm))
                link(nc.vector.tensor_copy(tab_cw[:, :, 0:N_EXP], cwe))
                link(nc.vector.tensor_copy(ftab[:, 1:], c("expert")))
                for j in range(ITEMS - N_EXP):
                    link(nc.vector.scalar_tensor_tensor(osel, exc, float(j), ov, ALU.is_equal, ALU.mult))
                    oj = osel.unsqueeze(1).to_broadcast(e16)
                    col = slice(N_EXP + j, N_EXP + j + 1)
                    for table, values in ((tab_rk, rkm), (tab_cw, cwe)):
                        link(nc.vector.tensor_tensor(prod, values, oj, ALU.mult))
                        link(nc.vector.tensor_reduce(table[:, :, col].rearrange("p t i -> p (t i)"), prod, AX, ALU.add))
                    link(nc.vector.tensor_tensor(wrb, osel, c("iota8"), ALU.mult))
                    link(nc.vector.tensor_reduce(ftab[:, 1 + N_EXP + j:2 + N_EXP + j], wrb, AX, ALU.add))
                link(nc.vector.tensor_scalar(tab_rk[:, :, N_EXP:ITEMS], tab_rk[:, :, N_EXP:ITEMS], float(-P), None, ALU.add))
                link(nc.vector.tensor_scalar(ftab[:, 1 + N_EXP:1 + ITEMS], ftab[:, 1 + N_EXP:1 + ITEMS], 1.0, None, ALU.add))
                link(nc.vector.tensor_scalar(ftab[:, 0:1], inc[:, N_EXP - 1:N_EXP], float(N_EXP), None, ALU.add))
                link(nc.vector.tensor_scalar(ftab, ftab, lay[:, 2:3], None, ALU.mult))
                link(nc.vector.scalar_tensor_tensor(ftab[:, 0:1], lay[:, 3:4], float(DENSE_ITEMS), ftab[:, 0:1], ALU.mult, ALU.add))
                nc.vector.tensor_copy(itab[:, 0:ITEM_COLS + 1], ftab).then_inc(s_tab, 1)
                link(nc.vector.tensor_scalar(item_rk[:, :, 1:], tab_rk[:, :, 1:], lay[:, 2:3], None, ALU.mult))
                link(nc.vector.scalar_tensor_tensor(item_rk[:, :, 1:], drk[:, :, 1:], lay[:, 3:4], item_rk[:, :, 1:], ALU.mult, ALU.add))
                link(nc.vector.tensor_scalar(item_cw[:, :, 1:], tab_cw, lay[:, 2:3], None, ALU.mult))
                link(nc.vector.tensor_scalar(item_cw[:, :, 1:], item_cw[:, :, 1:], lay[:, 3:4], None, ALU.add))

                def gathered_lo(index):
                    for b in range(2):
                        dve.wait_ge(s_xh, index * 2 + (b + 1))
                        nc.vector.tensor_tensor(x_lo[:, 4 * b:4 * b + 4, :],
                                                ps[:, 1 + 2 * b, :].rearrange("p (k n) -> p k n", k=4),
                                                x_hi[:, 4 * b:4 * b + 4, :].bitcast(F32), ALU.subtract).then_inc(s_xl, 1)

                def add_item(index, i):
                    for q, bank in enumerate(SCATTER_BANKS):
                        t, half = q // 2, q % 2
                        dve.wait_ge(s_cb, index * 4 + (q + 1))
                        part_y = cat[:, t, 512 * half:512 * half + 512]
                        nc.vector.scalar_tensor_tensor(part_y, ps[:, bank, :], item_cw[:, t, bass.ds(i, 1)], part_y,
                                                       ALU.mult, ALU.add).then_inc(s_ac, 1)

                gathered_lo(l * (DENSE_ITEMS + 1))
                hold(dve, s_tab, l + 1)
                n_items = dve.value_load(itab[0:1, 0:1], min_val=2, max_val=ITEMS)
                with dve.Fori(0, n_items) as i:
                    item = l * DENSE_ITEMS + i
                    inb = l * LAYER_UNITS + i * ITEM_UNITS + MIX_UNITS
                    it7 = item * FC

                    def gate_silu(count, f_par):
                        dve.wait_ge(s_sig, count)
                        nc.vector.tensor_tensor(gsig[:], ps[:, f_par, :], sig[:], ALU.mult).then_inc(s_gs, 1)

                    def hidden(count, ub, u_done, f_par):
                        dve.wait_ge(s_used, ub + (u_done + RING + 1))
                        dve.wait_ge(s_gs, count)
                        nc.vector.tensor_tensor(hid[:], ps[:, 2 + f_par, :], gsig[:], ALU.mult).then_inc(s_hd, 1)

                    def hidden_lo(count):
                        dve.wait_ge(s_th, count)
                        nc.vector.tensor_tensor(hid_lo[:], ps[:, 6, :].rearrange("p (k n) -> p k n", k=4),
                                                hid_hi[:].bitcast(F32), ALU.subtract).then_inc(s_tl, 1)

                    split(inb, 3)
                    split(inb, 4)
                    gate_silu(it7 + 1, 0)
                    split(inb, 5)
                    add_item(item + l, i)
                    split(inb, 6)
                    hidden(it7 + 1, inb, 3, 0)
                    dve.wait_ge(s_sT, item + 1)
                    gather_matrix(i + 1)
                    with dve.Fori(0, FC // 2) as j:
                        jnb = inb + j * 12
                        for u in range(2):
                            k0 = 4 + 6 * u
                            done = it7 + j * 2 + u
                            split(jnb, k0 + 3)
                            split(jnb, k0 + 4)
                            hidden_lo(done + 1)
                            gate_silu(done + 2, (u + 1) % 2)
                            split(jnb, k0 + 5)
                            split(jnb, k0 + 6)
                            hidden(done + 2, jnb, k0 + 3, (u + 1) % 2)
                            split(jnb, k0 + 7)
                            split(jnb, k0 + 8)
                    hidden_lo(it7 + FC)
                    gathered_lo(item + l + 1)
                    split(inb, ITEM_UNITS + 1)
                    dve.wait_ge(s_used, inb + (ITEM_UNITS - 1 + RING + 1))
                    nc.vector.tensor_copy(d_sb[:, 512:1024], ps[:, 5, :]).then_inc(s_dV, 1)
                    split(inb, ITEM_UNITS + 2)
                last = l * DENSE_ITEMS + l + n_items
                add_item(last, n_items)
                for t in range(TILES):
                    for b in range(2):
                        dve.wait_ge(s_ac, last * 4 + (2 * t + b + 1))
                        statistics(cat, t, b)
                normalise(l * 4 + 4, l * 2 + 2, cat)
                transposed_lo(l * 4 + 4, act_hi, act_lo)
                assert link_count[1] == DVE_LAYER, link_count[1]

        @block.tensor
        def _(pe):
            def product(dst, xh, xl, wh, wl, start, stop):
                nc.tensor.matmul(dst, xh, wh, start=start, stop=False)
                nc.tensor.matmul(dst, xh, wl, start=False, stop=False)
                return nc.tensor.matmul(dst, xl, wh, start=False, stop=stop)

            def unit(nb, k, banks, kts, width, hi, lo, first, last):
                pe.wait_ge(s_lo, nb + (k + 1))
                for t, bank in enumerate(banks):
                    for j, kt in enumerate(kts):
                        ins = product(ps[:, bank, 0:width], hi[:, kt, t * P:t * P + P], lo[:, kt, t * P:t * P + P],
                                      w_hi[:, k % HRING, j * width:(j + 1) * width],
                                      w_lo[:, k % RING, j * width:(j + 1) * width],
                                      first and j == 0, last and j == len(kts) - 1)
                ins.then_inc(s_used, 1)

            def transposes(wait, src, steps=range(4), layout=JOB):
                for step in steps:
                    t, half, bank = layout[step]
                    wait(t)
                    for b in range(4):
                        o = 512 * half + P * b
                        ins = nc.tensor.transpose(ps[:, bank, b * P:b * P + P], src[:, t, o:o + P], ident)
                    ins.then_inc(s_tp, 1)

            nc.tensor.sem_inc(s_used, RING)
            pe.wait_ge(s_cst, 16)
            pe.wait_ge(s_zero, 1)
            transposes(lambda t: pe.wait_ge(s_h, t + 1), h)

            with pe.Fori(0, DEPTH) as l:
                nb = l * LAYER_UNITS

                def qk_transposes(j, wait_stage):
                    cc, slot, nblk = [(0, 0, 4), (1, 1, 4), (3, 0, 4), (4, 1, 2), (5, 0, 2)][j]
                    wait_stage()
                    if j:
                        pe.wait_ge(s_qte, l * 5 + j)
                    for t in range(TILES):
                        for b in range(nblk):
                            ins = nc.tensor.transpose(ps[:, 4 + t, b * P:b * P + P],
                                                      q_stage[:, slot, t, b * P:b * P + P], ident)
                    ins.then_inc(s_qt, 1)

                pe.wait_ge(s_tpl, l * 16 + 4)
                for cc in range(6):
                    if cc in (2, 3):
                        pe.wait_ge(s_rope, l * 4 + 2 * (cc - 1))
                    if cc in (4, 5):
                        pe.wait_ge(s_qev, l * 4 + (cc - 3))
                    b = 2 * (cc % 2)
                    for hk in range(2):
                        unit(nb, 2 * cc + hk, (b, b + 1), range(4 * hk, 4 * hk + 4), 512, act_hi, act_lo, hk == 0, hk == 1)
                    if cc == 1:
                        qk_transposes(0, lambda: pe.wait_ge(s_rope, l * 4 + 2))
                    if cc == 2:
                        qk_transposes(1, lambda: pe.wait_ge(s_rope, l * 4 + 4))
                    if cc == 4:
                        qk_transposes(2, lambda: pe.wait_ge(s_qev, l * 4 + 2))
                    if cc == 5:
                        qk_transposes(3, lambda: pe.wait_ge(s_qev, l * 4 + 3))
                for hk in range(2):
                    unit(nb, U_F + hk, (6, 7), range(4 * hk, 4 * hk + 4), NF, act_hi, act_lo, hk == 0, hk == 1)
                qk_transposes(4, lambda: pe.wait_ge(s_qev, l * 4 + 4))

                def scores(g):
                    kind, t = GROUPS[g]
                    m, keys = groups_of(kind, t)
                    if g == 0:
                        pe.wait_ge(s_qte, l * 5 + 5)
                    else:
                        pe.wait_ge(s_scr, l * 6 + FREED_BY[g])
                    if kind == "fox" and g == 2:
                        pe.wait_ge(s_Fr, l + 1)
                    z = scores_of(g)
                    for j in range(m):
                        blk, r = j // 2, HD * (j % 2)
                        pos = place_of(g, j)
                        o = pos % (m // 2) * keys
                        dst = z[:, pos // (m // 2), o:o + keys]
                        q = qkT[r:r + HD, Q_BLK[kind] + blk, t * P:t * P + P]
                        k = qkT[r:r + HD, K_BLK[kind] + blk, 0:keys]
                        ins = nc.tensor.matmul(dst, q, k, start=True, stop=kind != "fox")
                        if kind == "fox":
                            a = COLS["negsel"][0] + j * P
                            ins = nc.tensor.matmul(dst, cst[0:NF, a:a + P], f_row[0:NF, 0:keys], start=False, stop=True)
                    ins.then_inc(s_sc, 1)

                def turn_weights(g):
                    kind, t = GROUPS[g]
                    m, keys = groups_of(kind, t)
                    buf = prob(g)
                    if kind == "sb":
                        pe.wait_ge(s_ex, l * 6 + (g + 1))
                    else:
                        pe.wait_ge(s_w, l * 4 + {0: 1, 2: 2, 3: 3, 5: 4}[g])
                    if g == 0:
                        pe.wait_ge(s_Fr, l + 1)
                        pe.wait_ge(s_Fc, l + 1)
                    else:
                        pe.wait_ge(s_pve, l * 6 + (g if t else g - 1))
                    for r in range(t + 1):
                        for hh in range(4):
                            o = (hh if kind == "diff" else place_of(g, hh)) * keys + r * P
                            ins = nc.tensor.transpose(ps[:, turned_bank(g, r), hh * P:hh * P + P], buf[:, o:o + P], ident)
                        ins.then_inc(s_wt, 1)

                def heads(g):
                    kind, t = GROUPS[g]
                    pe.wait_ge(s_wte, l * ROUNDS + (ROUNDS_BEFORE[g] + t + 1))
                    width = P if kind == "diff" else HD
                    for hh in range(4):
                        for r in range(t + 1):
                            v0 = CAT_OFF[kind] + hh * width
                            ins = nc.tensor.matmul(ps[:, heads_bank(g), hh * width:(hh + 1) * width],
                                                   wT[:, turned_bank(g, r) - 6, hh, :],
                                                   v_sb[:, r, v0:v0 + width], start=(r == 0), stop=(r == t))
                    ins.then_inc(s_pv, 1)

                def gate_unit(g, hk):
                    unit(nb, U_GATE + 2 * g + hk, (0, 1), range(4 * hk, 4 * hk + 4), 512, act_hi, act_lo, hk == 0, hk == 1)

                gate_unit(0, 0)
                scores(0)
                gate_unit(0, 1)
                pe.wait_ge(s_lf, l + 1)
                for k in range(TILES):
                    nc.tensor.matmul(ps[0:NF, 6, 0:SEQ], lf[:, k, :], tri[:, k, :], start=(k == 0), stop=(k == TILES - 1))
                nc.tensor.matmul(ps[:, 7, 0:NF], tri[:, 0, 0:P], lf[:, 0, :], start=True, stop=True)
                for k in range(TILES):
                    ins = nc.tensor.matmul(ps[:, 7, NF:2 * NF], tri[:, k, P:2 * P], lf[:, k, :],
                                           start=(k == 0), stop=(k == TILES - 1))
                ins.then_inc(s_F, 1)
                scores(1)
                for g in range(1, 6):
                    pe.wait_ge(s_gl, l * 6 + g)
                    gate_unit(g, 0)
                    if g >= 2:
                        heads(g - 2)
                    gate_unit(g, 1)
                    if g < 5:
                        scores(g + 1)
                    turn_weights(g - 1)

                def wait_tile1(t):
                    pe.wait_ge(s_pve, l * 6 + 3)
                    pe.wait_ge(s_rms, l * 2 + 1)
                    pe.wait_ge(s_scr, l * 6 + 5)

                def wait_diff0(t):
                    pe.wait_ge(s_rms, l * 2 + 2)
                    pe.wait_ge(s_scr, l * 6 + 6)

                transposes(wait_tile1, cat, (0, 1), HEADS_JOB)
                turn_weights(5)
                heads(4)
                transposes(wait_diff0, cat, (2,), HEADS_JOB)
                heads(5)
                transposes(lambda t: pe.wait_ge(s_pve, l * 6 + 6), cat, (3,), HEADS_JOB)
                pe.wait_ge(s_tpl, l * 16 + 8)
                pe.wait_ge(s_gl, l * 6 + 6)
                for cc in range(2):
                    for b in range(3):
                        if cc:
                            pe.wait_ge(s_gm, l * 6 + (b + 1))
                        k0, n = ((0, 4), (4, 2), (6, 2))[b]
                        if cc and b == 2:
                            transposes(lambda t: pe.wait_ge(s_mrg, l * 4 + 2), cat, (0, 1), MERGED_JOB)
                        unit(nb, U_UP + 3 * cc + b, (2 * b, 2 * b + 1), range(k0, k0 + n), 512, act_hi, act_lo, True, True)

                def out_unit(hk, cc):
                    unit(nb, U_OUT + 2 * hk + cc, (2 * cc, 2 * cc + 1), range(4 * hk, 4 * hk + 4), 512, mrg_hi, mrg_lo, hk == 0, hk == 1)

                pe.wait_ge(s_tpl, l * 16 + 10)
                pe.wait_ge(s_gm, l * 6 + 4)
                out_unit(0, 0)
                transposes(lambda t: pe.wait_ge(s_mrg, l * 4 + 4), cat, (2, 3), MERGED_JOB)
                out_unit(0, 1)
                pe.wait_ge(s_tpl, l * 16 + 12)
                out_unit(1, 0)
                out_unit(1, 1)
                transposes(lambda t: pe.wait_ge(s_h, l * 4 + (TILES + t + 1)), h)

                pe.wait_ge(s_tpl, l * 16 + 16)
                pe.wait_ge(s_wrl, l + 1)
                for kt in range(KT):
                    for a, part in enumerate((act_hi, act_lo)):
                        for b, weights in enumerate((wr_hi, wr_lo)):
                            ins = nc.tensor.matmul(ps[0:N_EXP, 6, 0:SEQ], weights[:, kt, :], part[:, kt, :],
                                                   start=(kt + a + b == 0), stop=(kt == KT - 1 and a + b == 2))
                ins.then_inc(s_lgr, 1)
                hold(pe, s_lgc, l + 1)
                for t in range(TILES):
                    ins = nc.tensor.matmul(ps[:, 7, N_EXP * t:N_EXP * t + N_EXP], lg_row[0:N_EXP, t * P:t * P + P],
                                           ident[0:N_EXP, 0:N_EXP], start=True, stop=True)
                ins.then_inc(s_lg, 1)
                pe.wait_ge(s_sel, l + 1)
                nc.tensor.matmul(ps[:, 6, 0:N_EXP], tri[:, 0, 0:P], sel[:, 0, :], start=True, stop=True)
                for k in range(TILES):
                    nc.tensor.matmul(ps[:, 6, N_EXP:2 * N_EXP], tri[:, k, P:2 * P], sel[:, k, :], start=(k == 0), stop=(k == TILES - 1))
                for k in range(TILES):
                    ins = nc.tensor.matmul(ps[:, 7, 0:N_EXP], tri[:, 0, P:2 * P], sel[:, k, :], start=(k == 0), stop=(k == TILES - 1))
                ins.then_inc(s_rk, 1)

                def gather(index):
                    pe.wait_ge(s_S, index + 1)
                    for b in range(2):
                        for j in range(4):
                            o = (4 * b + j) * P
                            for t in range(TILES):
                                ins = nc.tensor.matmul(ps[:, 1 + 2 * b, j * P:j * P + P], h[:, t, o:o + P], gath[:, t, :],
                                                       start=(t == 0), stop=(t == TILES - 1))
                        ins.then_inc(s_ga, 1)

                def scatter(index, item_count):
                    pe.wait_ge(s_dA, item_count + 1)
                    pe.wait_ge(s_dV, item_count + 1)
                    pe.wait_ge(s_sTe, item_count + 1)
                    for q, bank in enumerate(SCATTER_BANKS):
                        t, half = q // 2, q % 2
                        nc.tensor.matmul(ps[:, bank, :], scat[:, t, :], d_sb[:, 512 * half:512 * half + 512],
                                         start=True, stop=True).then_inc(s_cb, 1)

                gather(l * (DENSE_ITEMS + 1))
                hold(pe, s_tab, l + 1)
                n_items = pe.value_load(itab[0:1, 0:1], min_val=2, max_val=ITEMS)
                with pe.Fori(0, n_items) as i:
                    item = l * DENSE_ITEMS + i
                    inb = l * LAYER_UNITS + i * ITEM_UNITS + MIX_UNITS
                    it7 = item * FC
                    sc_index = item + l

                    def proj(ub, k, bank):
                        for hk in range(2):
                            unit(ub, k + hk, (bank,), range(4 * hk, 4 * hk + 4), 512, x_hi, x_lo, hk == 0, hk == 1)

                    def turn_hidden(count):
                        pe.wait_ge(s_hd, count)
                        for b in range(4):
                            ins = nc.tensor.transpose(ps[:, 6, b * P:b * P + P], hid[:, b * P:b * P + P], ident)
                        ins.then_inc(s_tr, 1)

                    def down(ub, k, count, last):
                        pe.wait_ge(s_tl, count)
                        for hk in range(2):
                            pe.wait_ge(s_lo, ub + (k + hk + 1))
                            for j in range(2):
                                for half in range(2):
                                    o = 1024 * j + 512 * half
                                    ins = product(ps[:, 4 + half, :], hid_hi[:, 2 * hk + j, :], hid_lo[:, 2 * hk + j, :],
                                                  w_hi[:, (k + hk) % HRING, o:o + 512], w_lo[:, (k + hk) % RING, o:o + 512],
                                                  False, last and hk == 1 and j == 1)
                            ins.then_inc(s_used, 1)

                    pe.wait_ge(s_xl, (item + l) * 2 + 2)
                    proj(inb, 0, 0)
                    proj(inb, 2, 2)
                    scatter(sc_index, item)
                    for half in range(2):
                        nc.tensor.matmul(ps[:, 4 + half, :], zero_w[:], x_hi[:, 0:4, :].rearrange("p k n -> p (k n)"), start=True, stop=False)
                    pe.wait_ge(s_gs, it7 + 1)
                    for t in range(TILES):
                        ins = nc.tensor.transpose(ps[:, 0, t * P:t * P + P], gath[:, t, :], ident)
                    ins.then_inc(s_sT, 1)
                    with pe.Fori(0, FC // 2) as j:
                        jnb = inb + j * 12
                        for u in range(2):
                            k0 = 4 + 6 * u
                            done = it7 + j * 2 + u
                            if u == 0:
                                pe.wait_ge(s_ac, sc_index * 4 + 1)
                            proj(jnb, k0, (u + 1) % 2)
                            if u == 0:
                                pe.wait_ge(s_sTe, item + 2)
                                pe.wait_ge(s_ac, sc_index * 4 + 4)
                            turn_hidden(done + 1)
                            proj(jnb, k0 + 2, 2 + (u + 1) % 2)
                            down(jnb, k0 + 4, done + 1, False)
                    turn_hidden(it7 + FC)
                    gather(item + l + 1)
                    down(inb, 4 + 6 * (FC - 1), it7 + FC, True)
                pe.wait_ge(s_xl, (l * (DENSE_ITEMS + 1) + n_items) * 2 + 2)
                scatter(l * (DENSE_ITEMS + 1) + n_items, l * DENSE_ITEMS + n_items)
                transposes(lambda t: pe.wait_ge(s_h, l * 4 + (2 * TILES + t + 1)), h)


def kernel(**inputs):
    import numpy as _np
    import concourse.bacc as _bacc
    from concourse import mybir as _mybir
    from concourse.bass_utils import run_bass_kernel_spmd as _run

    a = {name: _np.asarray(value) for name, value in inputs.items()}
    sent = {
        "x": a["x"],
        "consts": constants(),
        "ln_in": _np.stack([a["ln_in_g"], a["ln_in_b"]]),
        "w_mix": mixer_stream(a["w_in"], a["w_up_diff"], a["w_up_sb"], a["w_up_fox"], a["w_out"]),
        "b_forget": a["b_forget"],
        "lam_qk": _np.stack([a["lam_q1"], a["lam_k1"], a["lam_q2"], a["lam_k2"]], axis=1),
        "diff_g": a["diff_norm_g"],
        "ln_mix": _np.stack([a["ln_mix_g"], a["ln_mix_b"]], axis=1),
        "ln_ffn": _np.stack([a["ln_ffn_g"], a["ln_ffn_b"]], axis=1),
        "w_router": a["w_router"],
        "b_router": a["b_router"],
        "w_item": item_stream(_np.concatenate([a["w_gate_dense"], a["w_gate_moe"][0]]),
                              _np.concatenate([a["w_up_dense"], a["w_up_moe"][0]]),
                              _np.concatenate([a["w_down_dense"], a["w_down_moe"][0]])),
    }
    nc = _bacc.Bacc("TRN2", target_bir_lowering=False, num_devices=1)
    arrays, args = {}, []
    for name, value in sent.items():
        value = _np.ascontiguousarray(value)
        arrays[f"in_{name}"] = value
        args.append(nc.dram_tensor(f"in_{name}", value.shape, _mybir.dt.from_np(value.dtype), kind="ExternalInput").ap())
    args.append(nc.dram_tensor("out_h", (1, SEQ, D), F32, kind="ExternalOutput").ap())
    build(nc, *args)
    r = _run(nc, [arrays], core_ids=[0])
    return r.results[0]["out_h"]
```
